# Optimizing a Trainium2 kernel written in Bass

```python
import math
import jax
import jax.numpy as jnp
from jax import lax
import numpy as np

D_MODEL = 1024
BATCH = 1
SEQ = 256
DEPTH = 1
DEC_BATCH = 8
DEC_SEQ = 1
PAST_LEN = 2048
PAGE_SIZE = 128

HEAD_DIM = 64
ATTN_SCALE = HEAD_DIM ** -0.5
MOBA_HEADS = 8
MOBA_BLOCK = 256
MOBA_TOPK = 3
MOBA_Q_BLOCK = 128
DIL_HEADS = 4
DILATIONS = (1, 4, 16)
DIL_STEPS = 128
DIL_WINDOWS = tuple(DIL_STEPS * d for d in DILATIONS)
DIL_BLOCK = 128
N_DIL = len(DILATIONS)
TOTAL_HEADS = MOBA_HEADS + N_DIL * DIL_HEADS
A_WIDTH = MOBA_HEADS * HEAD_DIM
B_WIDTH = N_DIL * DIL_HEADS * HEAD_DIM
B_OUT = DIL_HEADS * HEAD_DIM
IN_SIZES = (A_WIDTH, A_WIDTH, A_WIDTH, B_WIDTH, B_WIDTH, B_WIDTH, D_MODEL, D_MODEL)
IN_OFFSETS = tuple(int(v) for v in np.cumsum(IN_SIZES)[:-1])
RPE_BUCKETS = 32
RPE_EXACT = RPE_BUCKETS // 2
RPE_MAX_DIST = 128
MOE_GROUPS = 4
MOE_EXPERTS_PER_GROUP = 8
MOE_EXPERTS = MOE_GROUPS * MOE_EXPERTS_PER_GROUP
MOE_TOP_K = 2
MOE_FF = 512
MOE_BLOCK = 128
ALPHA = (2 * DEPTH) ** 0.25
BETA = (8 * DEPTH) ** -0.25
LN_EPS = 1e-5

kernel_name = 'hybrid_moba_dilated_hmoe_decode_step'

def _normalize(x):
    xf = x.astype(jnp.float32)
    mu = xf.mean(-1, keepdims=True)
    var = jnp.square(xf - mu).mean(-1, keepdims=True)
    return ((xf - mu) * lax.rsqrt(var + LN_EPS)).astype(x.dtype)

def _layer_norm(x, g, b):
    return (_normalize(x).astype(jnp.float32) * g + b).astype(x.dtype)

def _adaln(c, w, b):
    m = jax.nn.silu(c) @ w + b
    return [t[:, None, :] for t in jnp.split(m, 6, axis=-1)]

def _rpe_bucket(dist):
    n = jnp.maximum(dist, 0)
    nf = jnp.maximum(n, 1).astype(jnp.float32)
    large = RPE_EXACT + (jnp.log(nf / RPE_EXACT) / math.log(RPE_MAX_DIST / RPE_EXACT)
                         * (RPE_BUCKETS - RPE_EXACT)).astype(jnp.int32)
    return jnp.where(n < RPE_EXACT, n, jnp.minimum(large, RPE_BUCKETS - 1))

def _mixer_inputs(x, shift, scale, w_in):
    h = _normalize(x) * (1 + scale) + shift
    qa, ka, va, qb, kb, vb, ga, gb = jnp.split(h @ w_in, IN_OFFSETS, axis=-1)
    hd = lambda t: t.reshape(t.shape[:-1] + (-1, HEAD_DIM))
    return hd(qa), hd(ka), hd(va), hd(qb), hd(kb), hd(vb), ga, gb

def _moba_seq(q, q_pos, k, v, tab):
    t_len, n_h, dh = q.shape
    k_len = k.shape[0]
    nb = -(-k_len // MOBA_BLOCK)
    pad = nb * MOBA_BLOCK - k_len
    kb = jnp.pad(k, ((0, pad), (0, 0), (0, 0))).reshape(nb, MOBA_BLOCK, n_h, dh).transpose(2, 0, 1, 3)
    vb = jnp.pad(v, ((0, pad), (0, 0), (0, 0))).reshape(nb, MOBA_BLOCK, n_h, dh).transpose(2, 0, 1, 3)
    means = kb.astype(jnp.float32).mean(axis=2)
    n_sel = min(MOBA_TOPK, nb)
    qc = min(MOBA_Q_BLOCK, t_len)
    nq = -(-t_len // qc)
    tp = nq * qc
    qp = jnp.pad(q, ((0, tp - t_len), (0, 0), (0, 0))).reshape(nq, qc, n_h, dh)
    pp = jnp.pad(q_pos, (0, tp - t_len), mode='edge').reshape(nq, qc)
    offs = jnp.arange(MOBA_BLOCK, dtype=jnp.int32)

    def chunk(args):
        qq, pos = args
        qh = qq.transpose(1, 0, 2)
        own = pos // MOBA_BLOCK
        s = jnp.einsum('hqd,hnd->hqn', qh.astype(jnp.float32), means)
        s = jnp.where(jnp.arange(nb)[None, None, :] < own[None, :, None], s, -jnp.inf)
        top_s, top_i = lax.top_k(s, n_sel)
        own_b = jnp.broadcast_to(own[None, :, None], (n_h, qc, 1))
        blocks = jnp.concatenate([top_i.astype(jnp.int32), own_b], axis=-1)
        blk_ok = jnp.concatenate([jnp.isfinite(top_s), jnp.ones((n_h, qc, 1), bool)], axis=-1)
        kg = jax.vmap(lambda t, i: t[i])(kb, blocks)
        vg = jax.vmap(lambda t, i: t[i])(vb, blocks)
        key_pos = blocks[..., None] * MOBA_BLOCK + offs
        dist = pos[None, :, None, None] - key_pos
        bias = jax.vmap(lambda tb, bk: tb[bk])(tab.T, _rpe_bucket(dist))
        logits = jnp.einsum('hqd,hqjkd->hqjk', qh, kg).astype(jnp.float32) * ATTN_SCALE + bias
        logits = jnp.where(blk_ok[..., None] & (dist >= 0), logits, -jnp.inf)
        p = jax.nn.softmax(logits.reshape(n_h, qc, -1), axis=-1).reshape(logits.shape)
        return jnp.einsum('hqjk,hqjkd->qhd', p.astype(v.dtype), vg)

    out = lax.map(chunk, (qp, pp))
    return out.reshape(tp, n_h, dh)[:t_len]

def _moba_prompt(q, k, v, tab):
    pos = jnp.arange(q.shape[1], dtype=jnp.int32)
    return lax.map(lambda a: _moba_seq(a[0], pos, a[1], a[2], tab), (q, k, v))

def _moba_sample(q, k_new, v_new, pages_k, pages_v, page_table, tab):
    past = page_table.shape[1] * pages_k.shape[1]
    pos = past + jnp.arange(q.shape[1], dtype=jnp.int32)
    n_h, dh = pages_k.shape[-2:]

    def one(a):
        qq, kn, vn, pt = a
        kp = pages_k[pt].reshape(past, n_h, dh)
        vp = pages_v[pt].reshape(past, n_h, dh)
        return _moba_seq(qq, pos, jnp.concatenate([kp, kn], 0), jnp.concatenate([vp, vn], 0), tab)

    return lax.map(one, (q, k_new, v_new, page_table))

def _dilated_prompt(q, k, v, d, tab):
    b, s, n_h, dh = q.shape
    ls = s // d
    nb = -(-ls // DIL_BLOCK)
    lp = nb * DIL_BLOCK

    def sub(x):
        x = x.reshape(b, ls, d, n_h, dh).transpose(0, 2, 1, 3, 4)
        return jnp.pad(x, ((0, 0), (0, 0), (0, lp - ls), (0, 0), (0, 0)))

    def band(x):
        x = jnp.pad(sub(x), ((0, 0), (0, 0), (DIL_BLOCK, 0), (0, 0), (0, 0)))
        x = x.reshape(b, d, nb + 1, DIL_BLOCK, n_h, dh)
        return jnp.concatenate([x[:, :, :-1], x[:, :, 1:]], axis=3)

    qs = sub(q).reshape(b, d, nb, DIL_BLOCK, n_h, dh)
    kw, vw = band(k), band(v)
    qi = jnp.arange(DIL_BLOCK, dtype=jnp.int32)
    kj = jnp.arange(2 * DIL_BLOCK, dtype=jnp.int32)
    steps = DIL_BLOCK + qi[:, None] - kj[None, :]
    key_idx = (jnp.arange(nb, dtype=jnp.int32)[:, None, None] - 1) * DIL_BLOCK + kj[None, None, :]
    allowed = (steps >= 0) & (steps <= DIL_STEPS) & (key_idx >= 0)
    bias = tab.T[:, _rpe_bucket(steps * d)]
    logits = jnp.einsum('bdnqhe,bdnkhe->bdnhqk', qs, kw).astype(jnp.float32) * ATTN_SCALE + bias[None, None, None]
    logits = jnp.where(allowed[None, None, :, None], logits, -jnp.inf)
    lse = jax.nn.logsumexp(logits, axis=-1)
    p = jnp.exp(logits - lse[..., None])
    o = jnp.einsum('bdnhqk,bdnkhe->bdnqhe', p.astype(v.dtype), vw)
    o = o.reshape(b, d, lp, n_h, dh)[:, :, :ls].transpose(0, 2, 1, 3, 4).reshape(b, s, n_h, dh)
    lse = lse.transpose(0, 1, 2, 4, 3).reshape(b, d, lp, n_h)[:, :, :ls].transpose(0, 2, 1, 3).reshape(b, s, n_h)
    return o, lse

def _dilated_sample(q, kv_all, n_buf, d, tab):
    t_len = q.shape[1]
    steps = jnp.arange(DIL_STEPS + 1, dtype=jnp.int32)
    idx = n_buf + jnp.arange(t_len, dtype=jnp.int32)[:, None] - steps[None, :] * d
    ok = idx >= 0
    kvg = kv_all[:, jnp.maximum(idx, 0)]
    bias = tab.T[:, _rpe_bucket(steps * d)]
    logits = jnp.einsum('bthe,btmhe->bhtm', q, kvg[:, :, :, 0]).astype(jnp.float32) * ATTN_SCALE + bias[None, :, None, :]
    logits = jnp.where(ok[None, None], logits, -jnp.inf)
    lse = jax.nn.logsumexp(logits, axis=-1)
    p = jnp.exp(logits - lse[..., None])
    o = jnp.einsum('bhtm,btmhe->bthe', p.astype(kv_all.dtype), kvg[:, :, :, 1])
    return o, lse.transpose(0, 2, 1)

def _combine_dilations(outs, lses):
    w = jax.nn.softmax(jnp.stack(lses).astype(jnp.float32), axis=0)
    o = jnp.einsum('gbsh,gbshe->bshe', w, jnp.stack(outs).astype(jnp.float32))
    return o.astype(outs[0].dtype).reshape(o.shape[:2] + (B_OUT,))

def _merge(oa, ob, ga, gb, w_pa, w_pb, w_o):
    ya = oa.reshape(oa.shape[:2] + (A_WIDTH,)) @ w_pa
    yb = ob @ w_pb
    return (jax.nn.sigmoid(ga) * ya + jax.nn.sigmoid(gb) * yb) @ w_o

def _hier_moe(h, w_rg, b_rg, w_re, b_re, w_eg, w_eu, w_ed):
    n = h.shape[0]
    hf = h.astype(jnp.float32)
    lg = hf @ w_rg.astype(jnp.float32) + b_rg
    pg = jax.nn.softmax(lg, axis=-1)
    grp = jnp.argmax(lg, axis=-1).astype(jnp.int32)
    p_grp = jnp.take_along_axis(pg, grp[:, None], axis=1)[:, 0]
    le = jnp.einsum('nd,gde->nge', hf, w_re.astype(jnp.float32)) + b_re
    le = jnp.take_along_axis(le, grp[:, None, None], axis=1)[:, 0]
    v2, i2 = lax.top_k(le, MOE_TOP_K)
    wt = p_grp[:, None] * jax.nn.softmax(v2, axis=-1)
    eid = grp[:, None] * MOE_EXPERTS_PER_GROUP + i2.astype(jnp.int32)
    a = n * MOE_TOP_K
    flat_e = eid.reshape(-1)
    flat_t = jnp.repeat(jnp.arange(n, dtype=jnp.int32), MOE_TOP_K)
    flat_w = wt.reshape(-1)
    order = jnp.argsort(flat_e)
    se = flat_e[order]
    counts = jnp.bincount(flat_e, length=MOE_EXPERTS)
    pc = (counts + MOE_BLOCK - 1) // MOE_BLOCK * MOE_BLOCK
    pad_end = jnp.cumsum(pc)
    pad_start = pad_end - pc
    start = jnp.cumsum(counts) - counts
    dest = pad_start[se] + jnp.arange(a, dtype=jnp.int32) - start[se]
    nblk = a // MOE_BLOCK + MOE_EXPERTS
    rows = nblk * MOE_BLOCK
    row_tok = jnp.full((rows,), n, jnp.int32).at[dest].set(flat_t[order])
    row_w = jnp.zeros((rows,), jnp.float32).at[dest].set(flat_w[order])
    blk_e = jnp.minimum(jnp.searchsorted(pad_end // MOE_BLOCK, jnp.arange(nblk), side='right'),
                        MOE_EXPERTS - 1).astype(jnp.int32)
    xpad = jnp.concatenate([h, jnp.zeros((1, h.shape[1]), h.dtype)], axis=0)
    xb = xpad[row_tok].reshape(nblk, MOE_BLOCK, h.shape[1])

    def expert_block(args):
        xblk, e = args
        return (jax.nn.silu(xblk @ w_eg[e]) * (xblk @ w_eu[e])) @ w_ed[e]

    yb = lax.map(expert_block, (xb, blk_e)).reshape(rows, h.shape[1])
    contrib = (yb.astype(jnp.float32) * row_w[:, None]).astype(h.dtype)
    return jnp.zeros((n + 1, h.shape[1]), h.dtype).at[row_tok].add(contrib)[:n]

def setup_inputs(seed: int = 0) -> dict:
    key = jax.random.key(seed)
    ks = iter(jax.random.split(key, 48))

    def nrm(shape, scale):
        return jax.random.normal(next(ks), shape, jnp.float32) * scale

    inv = D_MODEL ** -0.5
    n_pages = PAST_LEN // PAGE_SIZE
    n_used = DEC_BATCH * n_pages
    n_phys = n_used + max(1, n_used // 4)
    page_table = jax.random.permutation(next(ks), n_phys)[:n_used].reshape(DEC_BATCH, n_pages).astype(jnp.int32)
    win_len = [min(w, PAST_LEN) for w in DIL_WINDOWS]
    w_in = jnp.concatenate([
        nrm((DEPTH, D_MODEL, A_WIDTH), inv), nrm((DEPTH, D_MODEL, A_WIDTH), inv),
        nrm((DEPTH, D_MODEL, A_WIDTH), inv * BETA),
        nrm((DEPTH, D_MODEL, B_WIDTH), inv), nrm((DEPTH, D_MODEL, B_WIDTH), inv),
        nrm((DEPTH, D_MODEL, B_WIDTH), inv * BETA),
        nrm((DEPTH, D_MODEL, D_MODEL), inv), nrm((DEPTH, D_MODEL, D_MODEL), inv)], axis=-1)
    return {
        'x_prompt': nrm((BATCH, SEQ, D_MODEL), 1.0),
        'x_sample': nrm((DEC_BATCH, DEC_SEQ, D_MODEL), 1.0),
        'cache_k_pages': nrm((DEPTH, n_phys, PAGE_SIZE, MOBA_HEADS, HEAD_DIM), 1.0),
        'cache_v_pages': nrm((DEPTH, n_phys, PAGE_SIZE, MOBA_HEADS, HEAD_DIM), 1.0),
        'page_table': page_table,
        'state_dil1_kv': nrm((DEPTH, DEC_BATCH, win_len[0], 2, DIL_HEADS, HEAD_DIM), 1.0),
        'state_dil4_kv': nrm((DEPTH, DEC_BATCH, win_len[1], 2, DIL_HEADS, HEAD_DIM), 1.0),
        'state_dil16_kv': nrm((DEPTH, DEC_BATCH, win_len[2], 2, DIL_HEADS, HEAD_DIM), 1.0),
        'c_prompt': nrm((BATCH, D_MODEL), 1.0),
        'c_sample': nrm((DEC_BATCH, D_MODEL), 1.0),
        'rel_bias': nrm((RPE_BUCKETS, TOTAL_HEADS), 0.3),
        'w_ada': nrm((DEPTH, D_MODEL, 6 * D_MODEL), 0.5 * inv),
        'b_ada': nrm((DEPTH, 6 * D_MODEL), 0.02),
        'w_in': w_in,
        'w_proj_a': nrm((DEPTH, A_WIDTH, D_MODEL), A_WIDTH ** -0.5 * BETA),
        'w_proj_b': nrm((DEPTH, B_OUT, D_MODEL), B_OUT ** -0.5 * BETA),
        'w_out': nrm((DEPTH, D_MODEL, D_MODEL), inv * BETA),
        'ln1_g': 1.0 + nrm((DEPTH, D_MODEL), 0.02),
        'ln1_b': nrm((DEPTH, D_MODEL), 0.02),
        'w_router_g': nrm((DEPTH, D_MODEL, MOE_GROUPS), inv),
        'b_router_g': nrm((DEPTH, MOE_GROUPS), 0.01),
        'w_router_e': nrm((DEPTH, MOE_GROUPS, D_MODEL, MOE_EXPERTS_PER_GROUP), inv),
        'b_router_e': nrm((DEPTH, MOE_GROUPS, MOE_EXPERTS_PER_GROUP), 0.01),
        'w_exp_gate': nrm((DEPTH, MOE_EXPERTS, D_MODEL, MOE_FF), inv * BETA),
        'w_exp_up': nrm((DEPTH, MOE_EXPERTS, D_MODEL, MOE_FF), inv * BETA),
        'w_exp_down': nrm((DEPTH, MOE_EXPERTS, MOE_FF, D_MODEL), MOE_FF ** -0.5 * BETA),
        'ln2_g': 1.0 + nrm((DEPTH, D_MODEL), 0.02),
        'ln2_b': nrm((DEPTH, D_MODEL), 0.02),
    }

def reference(x_prompt, x_sample, cache_k_pages, cache_v_pages, page_table, state_dil1_kv, state_dil4_kv,
              state_dil16_kv, c_prompt, c_sample, rel_bias, w_ada, b_ada, w_in, w_proj_a, w_proj_b, w_out,
              ln1_g, ln1_b, w_router_g, b_router_g, w_router_e, b_router_e, w_exp_gate, w_exp_up, w_exp_down,
              ln2_g, ln2_b):
    bsz, seq, d_model = x_prompt.shape
    dseq = x_sample.shape[1]
    tab_a = rel_bias[:, :MOBA_HEADS]
    tab_b = [rel_bias[:, MOBA_HEADS + g * DIL_HEADS: MOBA_HEADS + (g + 1) * DIL_HEADS] for g in range(N_DIL)]
    dil_states = (state_dil1_kv, state_dil4_kv, state_dil16_kv)
    xp, xs = x_prompt, x_sample
    kp_l, vp_l, ks_l, vs_l = [], [], [], []
    dp_l = [[] for _ in DILATIONS]
    ds_l = [[] for _ in DILATIONS]
    for l in range(DEPTH):
        mod_p = _adaln(c_prompt, w_ada[l], b_ada[l])
        mod_s = _adaln(c_sample, w_ada[l], b_ada[l])

        qa, ka, va, qb, kb, vb, ga, gb = _mixer_inputs(xp, mod_p[0], mod_p[1], w_in[l])
        oa = _moba_prompt(qa, ka, va, tab_a)
        outs, lses = [], []
        for g, d in enumerate(DILATIONS):
            hs = slice(g * DIL_HEADS, (g + 1) * DIL_HEADS)
            o, lse = _dilated_prompt(qb[:, :, hs], kb[:, :, hs], vb[:, :, hs], d, tab_b[g])
            outs.append(o)
            lses.append(lse)
            keep = min(DIL_WINDOWS[g], seq)
            dp_l[g].append(jnp.stack([kb[:, seq - keep:, hs], vb[:, seq - keep:, hs]], axis=2))
        mix = _merge(oa, _combine_dilations(outs, lses), ga, gb, w_proj_a[l], w_proj_b[l], w_out[l])
        xp = _layer_norm(ALPHA * xp + mod_p[2] * mix, ln1_g[l], ln1_b[l])
        kp_l.append(ka)
        vp_l.append(va)

        qa, ka, va, qb, kb, vb, ga, gb = _mixer_inputs(xs, mod_s[0], mod_s[1], w_in[l])
        oa = _moba_sample(qa, ka, va, cache_k_pages[l], cache_v_pages[l], page_table, tab_a)
        outs, lses = [], []
        for g, d in enumerate(DILATIONS):
            hs = slice(g * DIL_HEADS, (g + 1) * DIL_HEADS)
            buf = dil_states[g][l]
            kv_all = jnp.concatenate([buf, jnp.stack([kb[:, :, hs], vb[:, :, hs]], axis=2)], axis=1)
            o, lse = _dilated_sample(qb[:, :, hs], kv_all, buf.shape[1], d, tab_b[g])
            outs.append(o)
            lses.append(lse)
            ds_l[g].append(kv_all[:, dseq:])
        mix = _merge(oa, _combine_dilations(outs, lses), ga, gb, w_proj_a[l], w_proj_b[l], w_out[l])
        xs = _layer_norm(ALPHA * xs + mod_s[2] * mix, ln1_g[l], ln1_b[l])
        ks_l.append(ka)
        vs_l.append(va)

        hp = _normalize(xp) * (1 + mod_p[4]) + mod_p[3]
        hsm = _normalize(xs) * (1 + mod_s[4]) + mod_s[3]
        tok = jnp.concatenate([hp.reshape(-1, d_model), hsm.reshape(-1, d_model)], axis=0)
        f = _hier_moe(tok, w_router_g[l], b_router_g[l], w_router_e[l], b_router_e[l],
                      w_exp_gate[l], w_exp_up[l], w_exp_down[l])
        fp = f[:bsz * seq].reshape(xp.shape)
        fs = f[bsz * seq:].reshape(xs.shape)
        xp = _layer_norm(ALPHA * xp + mod_p[5] * fp, ln2_g[l], ln2_b[l])
        xs = _layer_norm(ALPHA * xs + mod_s[5] * fs, ln2_g[l], ln2_b[l])

    return (xp, xs, jnp.stack(kp_l), jnp.stack(vp_l), jnp.stack(ks_l), jnp.stack(vs_l),
            jnp.stack(dp_l[0]), jnp.stack(ds_l[0]), jnp.stack(dp_l[1]), jnp.stack(ds_l[1]),
            jnp.stack(dp_l[2]), jnp.stack(ds_l[2]))


_drawn_inputs = setup_inputs


def setup_inputs(seed=0):
    import zlib

    import numpy as np

    out = dict(_drawn_inputs(seed))
    spreads = {}
    factors = {'cache_k_pages': 8.0,
     'cache_v_pages': 8.0,
     'rel_bias': 8.0,
     'w_proj_a': 5.044,
     'w_proj_b': 5.986,
     'w_out': 3.713,
     'ln1_g': 2.848,
     'ln1_b': 2.8,
     'w_router_g': 4.373,
     'b_router_g': 8.0,
     'w_router_e': 4.207,
     'b_router_e': 8.0,
     'w_exp_gate': 3.821,
     'w_exp_up': 3.672,
     'w_exp_down': 3.65,
     'ln2_g': 2.844,
     'ln2_b': 2.853}
    for name, (base, spread) in spreads.items():
        noise = np.random.default_rng([zlib.crc32(name.encode()), seed]).standard_normal(out[name].shape)
        drawn = base * np.exp(spread * noise) if base else spread * noise
        out[name] = jnp.asarray(drawn.astype(out[name].dtype))
    for name, factor in factors.items():
        out[name] = (out[name] * factor).astype(out[name].dtype)
    return out
```

```python
from contextlib import ExitStack

import concourse.bass as bass
from concourse import mybir

F32 = mybir.dt.float32
I32 = mybir.dt.int32
U32 = mybir.dt.uint32
ALU = mybir.AluOpType
ACT = mybir.ActivationFunctionType
AX = mybir.AxisListType

P = 128
DM = 1024
KC = DM // P
SEQ = 256
NB = 8
NT = SEQ + NB
TT = [(0, P), (P, P), (SEQ, NB)]
HD = 64
HA = 8
HB = 4
DIL = (1, 4, 16)
NG = len(DIL)
HS = HA + HB
HALL = HA + NG * HB
AW = HA * HD
BW = NG * HB * HD
PAST = 2048
PAGE = 128
NPG = PAST // PAGE
HPG = NPG // 2
NBLK = 8
TOPK = 3
QSCALE = HD ** -0.5
BUCKETS = 32
VLEN = 384
NE = 32
EG = 8
NGRP = 4
FF = 512
FC = FF // P
SLOT = 64
MAXR = -(-NT // SLOT)
EPS = 1e-5
ALPHA = 2 ** 0.25
NEG = -1e30

QA, KA, VA, QB, KB, VB, GA, GB = 0, 4, 8, 12, 18, 24, 30, 38
C_ID, C_TRI, C_ONE, C_IOTA, C_IE, C_E96, C_H96, C_BD, C_TIE, C_HIND, C_TOK = (
    0, 128, 256, 384, 448, 480, 488, 500, 1012, 1076, 1078)
C_END = 1081
NX = MAXR * NE + 1
O_TOE, O_SMP, O_ZERO = 0, 4 * VLEN, 4 * VLEN + (NPG + NG) * P
O_END = O_ZERO + 8


def trunk(nc, x_prompt, x_sample, k_pages, v_pages, page_table, st1, st4, st16, c_prompt, c_sample,
          rel_bias, w_ada, b_ada, w_in, w_proj_a, w_proj_b, w_out, ln1_g, ln1_b, w_rg, b_rg, w_re,
          b_re, w_eg, w_eu, w_ed, ln2_g, ln2_b, consts, onehots, negrow,
          y_prompt, y_sample, k_prompt, v_prompt, k_sample, v_sample,
          d1p, d1s, d4p, d4s, d16p, d16s):
    ctx = ExitStack()
    with ctx:
        def sb(name, shape, dt=F32):
            return ctx.enter_context(nc.sbuf_tensor(name, shape, dt))

        def sem(name):
            return ctx.enter_context(nc.semaphore(name))

        def part(t, a, n, **shape):
            return t[:, a:a + n]

        cst = sb("cst", [P, C_END])
        ident, tri, ones = (cst[:, c:c + P] for c in (C_ID, C_TRI, C_ONE))
        iota = cst[:, C_IOTA:C_IOTA + SLOT]
        iota_e = cst[:, C_IE:C_IE + NE]
        e96 = cst[0:96, C_E96:C_E96 + NB]
        h96 = cst[0:96, C_H96:C_H96 + HS]
        blkdiag = cst[:, C_BD:C_BD + AW]
        tie = cst[:, C_TIE:C_TIE + 64]
        hind = cst[:, C_HIND:C_HIND + 2]

        ring = sb("ring", [P, 6, 4096])
        x = sb("x", [P, 3, DM])
        mod = sb("mod", [P, 48, NB + 1])
        bT = sb("bT", [P, 48])
        gates = sb("gates", [P, 16 * NT])
        zT = sb("zT", [P, 20 * NT])
        v = sb("v", [P, 3, AW + BW])
        hT = sb("hT", [P, KC * NT])
        qbc = sb("qbc", [P, 4 * AW])
        S = sb("S", [P, NB * NPG * HA])
        Sd = sb("Sd", [P, NB * NG * HB])
        qrep = sb("qrep", [P, 2, 4, P])
        work = sb("work", [P, 4 * NG * SEQ])
        cT = sb("cT", [P, KC * (NB + 1)])
        hs = sb("hs", [P, KC * NB])
        prod = sb("prod", [P, 10 * NB])
        own = sb("own", [NB, 64])
        m12 = sb("m12", [P, NB * HS])
        ownD = sb("ownD", [NB, NB * HS])
        st96 = sb("st96", [P, 128])
        powD = sb("powD", [NB, NB * HA + NB * NG * HB])
        rinv = sb("rinv", [NB, 2 * NB])
        rel = sb("rel", [BUCKETS + 1, HALL])
        sbias = sb("sbias", [P, NPG * HA + NG * HB])
        pt = sb("pt", [1, NB * NPG], I32)
        stat = sb("stat", [P, 24])
        nst = sb("nst", [P, 3, 2])
        sdev = sb("sdev", [P, 3])
        rounds_i = sb("rounds_i", [1, 1], I32)
        rowf = sb("rowf", [P, 2, 4])
        ridx = sb("ridx", [SLOT, 2], U32)
        wts = sb("wts", [P, 3, 2])

        hot = gates[0:BUCKETS + 1, 0:O_END]
        crow, brow_t = work[0:NB + 1, 0:DM], work[0:48, DM:DM + P]
        toev = work[0:HA, 1280:1280 + 4 * VLEN].rearrange("p (n w) -> p n w", n=4)
        kst = [work[:, i * 1280:(i + 1) * 1280] for i in range(2)]
        hT3 = hT[:, :].rearrange("p (k n) -> p k n", k=KC)
        zT3 = zT[:, :].rearrange("p (c n) -> p c n", n=NT)
        oT3 = qbc[:, 0:6 * NT].rearrange("p (c n) -> p c n", n=NT)
        gates3 = gates[:, :].rearrange("p (c n) -> p c n", n=NT)
        toe_a = hT[:, 0:HA * SEQ].rearrange("p (h k) -> p h k", k=SEQ)
        toe_b = x[:, :, :].rearrange("p a b -> p (a b)").rearrange("p (h k) -> p h k", k=SEQ)
        mixT = zT3[:, 0:KC, :]
        lng, lnb, g2p = (zT[:, 8 * NT + i * DM:8 * NT + (i + 1) * DM] for i in range(3))
        g2s = qbc[0:NB, 0:DM]
        pk = [work[:, i * 768:(i + 1) * 768] for i in range(2)]
        pT = [work[:, 1536 + i * 768:1536 + (i + 1) * 768] for i in range(2)]
        S4 = S[:, :].rearrange("p (b k h) -> p b k h", b=NB, k=NPG)
        Sd4 = Sd[:, :].rearrange("p (b g h) -> p b g h", b=NB, g=NG)
        h2 = v[:, :, 0:DM]
        xT = [gates[:, i * 512:(i + 1) * 512].rearrange("p (k n) -> p k n", k=KC) for i in range(2)]
        aT = [gates[:, 1024 + i * 256:1280 + i * 256] for i in range(2)]
        sg = [gates[:, 1536 + i * 256:1792 + i * 256] for i in range(2)]
        yT = [gates[:, 2048 + i * 512:2560 + i * 512].rearrange("p (k n) -> p k n", k=KC) for i in range(2)]
        G = [gates[:, 3072 + i * 192:3264 + i * 192].rearrange("p (t n) -> p t n", t=3) for i in range(2)]
        yrow = [work[0:SLOT, i * DM:(i + 1) * DM] for i in range(2)]
        posx, rowx = (S[:, i * 3 * NX:(i + 1) * 3 * NX].rearrange("p (t e) -> p t e", t=3) for i in range(2))

        bank = [ctx.enter_context(nc.psum_tensor(f"bank{i}", [P, 512], F32)) for i in range(8)]
        full = [sem(f"bank{i}_full") for i in range(8)]
        free = [sem(f"bank{i}_free") for i in range(8)]

        toe_d = nc.dram_tensor("toe_scratch", [HALL * VLEN], F32)
        ys_d = nc.dram_tensor("expert_rows", [2 * NT, DM], F32)

        (s_cst, s_hot, s_c, s_bt, s_x, s_pt, s_x2, s_silu, s_cT, s_bT, s_norm, s_mod, s_hTp, s_hs, s_hTs,
         s_z, s_qrep, s_qbc, s_kst, s_vout, s_vrow, s_toev, s_toes, s_toeb, s_toea, s_kmul, s_kred, s_prod,
         s_own, s_kdmul, s_kdred, s_sbias, s_pen, s_m12, s_ownx, s_negm, s_sub, s_exp, s_sum, s_rec, s_rs,
         s_ov, s_vm, s_vt, s_oa, s_pst, s_lg, s_pexp, s_pn, s_pT, s_po, s_u, s_mix, s_x1, s_ln1, s_ln2, s_n2,
         s_h2T, s_h2, s_wr, s_rb, s_rlg, s_rexp, s_rden, s_mask, s_wts, s_round, s_ridx, s_G, s_xg, s_xT, s_gu, s_sg,
         s_act, s_yt, s_yT, s_yb, s_yrow, s_g2, s_gat, s_y, s_out, s_st, s_dve, s_act_c, s_pool, s_moe,
         s_sc, s_scat, s_big, s_idx, s_var, s_sd, *s_vread) = [sem(n) for n in (
            "s_cst s_hot s_c s_bt s_x s_pt s_x2 s_silu s_cT s_bT s_norm s_mod s_hTp s_hs s_hTs "
            "s_z s_qrep s_qbc s_kst s_vout s_vrow s_toev s_toes s_toeb s_toea s_kmul s_kred s_prod "
            "s_own s_kdmul s_kdred s_sbias s_pen s_m12 s_ownx s_negm s_sub s_exp s_sum s_rec s_rs "
            "s_ov s_vm s_vt s_oa s_pst s_lg s_pexp s_pn s_pT s_po s_u s_mix s_x1 s_ln1 s_ln2 s_n2 "
            "s_h2T s_h2 s_wr s_rb s_rlg s_rexp s_rden s_mask s_wts s_round s_ridx s_G s_xg s_xT s_gu s_sg "
            "s_act s_yt s_yT s_yb s_yrow s_g2 s_gat s_y s_out s_st s_dve s_act_c s_pool s_moe "
            "s_sc s_scat s_big s_idx s_var s_sd s_vread0 s_vread1").split()]
        s_kout = [sem("s_kout0"), sem("s_kout1")]
        s_yst = [sem("s_yst0"), sem("s_yst1")]
        w_full = [sem(f"w_full{i}") for i in range(6)]
        ew_full = [sem(f"ew_full{i}") for i in range(6)]

        turn, uses = {}, [0] * 8

        def chain(eng, s):
            n = [0]

            def link(ins):
                n[0] += 1
                ins.then_inc(s, 1)
                eng.wait_ge(s, n[0])
            return link

        ring_use, slot_n, slot_v = {}, [0] * 6, [0] * 6

        def ring_take(name, slot, dmas=1):
            slot_v[slot] += 16 * dmas
            ring_use[name] = (slot, slot_n[slot], slot_v[slot])
            slot_n[slot] += 1

        weights = [("ada", t) for t in range(4)] + [("win", t) for t in range(12)] \
            + [("ada", t) for t in range(4, 12)] + [("wpa", 0), ("wpb", 0), ("wo", 0), ("wo", 1)]
        for n, name in enumerate(weights):
            ring_take(name, n % 4)
        for b in range(NB):
            ring_take(("k", b, 0), 4, HPG)
            ring_take(("k", b, 1), 5, HPG)
        for g in range(NG):
            ring_take(("kd", g), 4 + g % 2)
        v_val0 = (slot_v[4], slot_v[5])
        for b in range(NB):
            ring_take(("v", b, 0), 4, HPG)
            ring_take(("v", b, 1), 5, HPG)
        ring_take(("vd", 0), 4, 2)
        ring_take(("vd", 2), 5)

        def slot_of(name):
            return ring_use[name][0]

        def landed(eng, name):
            slot, _, val = ring_use[name]
            eng.wait_ge(w_full[slot], val)
            return ring[:, slot, :]

        last_use = {}

        def filled(eng, key):
            b, n = turn[key]
            eng.wait_ge(full[b], n + 1)
            return bank[b]

        states, st_out, st_p = (st1, st4, st16), (d1s, d4s, d16s), (d1p, d4p, d16p)
        V_TILES = {2: (0, 512), 6: (AW, 512), 7: (AW + 512, 256)}
        Q_AFTER = {0: (0, 1, 2, 3), 3: (4,), 5: (5,), 6: (6,), 7: (7,)}
        ZROW = {c: n for n, c in enumerate([*range(QA, VA), *range(QB, VB)])}
        KT = ((ZROW[KA], 4, 0), (ZROW[KB], 3, AW), (ZROW[KB + 3], 3, AW + 384))
        units = [("a", h, qt) for h in range(HA) for qt in range(2)] + \
                [("b", h, qt) for h in range(HB) for qt in range(2)]

        def heads(u):
            kind, h, _ = u
            if kind == "a":
                return [(ZROW[QA] + h // 2, ZROW[KA] + h // 2, h % 2, h * HD)]
            return [(ZROW[QB] + (g * HB + h) // 2, ZROW[KB] + (g * HB + h) // 2, h % 2, AW + (g * HB + h) * HD)
                    for g in range(NG)]

        block = ctx.enter_context(nc.Block())

        @block.tensor
        def _(pe):
            mm, tr = nc.tensor.matmul, nc.tensor.transpose

            def take(key, b):
                turn[key] = (b, uses[b])
                if uses[b]:
                    pe.wait_ge(free[b], uses[b])
                uses[b] += 1
                return bank[b]

            def done(key, ins):
                ins.then_inc(full[turn[key][0]], 1)

            pe.wait_ge(s_cst, 16)
            pe.wait_ge(s_silu, 1)
            bk = take("cT", 2)
            for k in range(KC):
                i = tr(bk[:, k * 9:(k + 1) * 9], crow[:, k * P:(k + 1) * P], ident[0:9, 0:9])
            done("cT", i)
            pe.wait_ge(s_bt, 16)
            bk = take("bT", 3)
            done("bT", tr(bk[:, 0:48], brow_t, ident[0:48, 0:48]))

            def ada(t):
                name = ("ada", t)
                w = landed(pe, name).rearrange("p (k n) -> p k n", k=KC)
                bk = take(name, t % 2)
                for j in range(4):
                    for k in range(KC):
                        i = mm(bk[:, j * 9:(j + 1) * 9], w[:, k, j * P:(j + 1) * P], cT[:, k * 9:(k + 1) * 9],
                               start=(k == 0), stop=(k == KC - 1))
                done(name, i)
                last_use[name] = name

            pe.wait_ge(s_cT, 1)
            for t in range(4):
                ada(t)

            for t, (t0, tn) in enumerate(TT):
                pe.wait_ge(s_norm, t + 1)
                for h in range(2):
                    bk = take(("xT", t, h), 2 + h)
                    for j in range(4):
                        k = 4 * h + j
                        i = tr(bk[:, j * P:j * P + tn], x[0:tn, t, k * P:(k + 1) * P], ident[0:tn, 0:tn])
                    done(("xT", t, h), i)

            pe.wait_ge(s_hot, 48)
            bk = take("sbias", 4)
            for p in range(NPG):
                mm(bk[:, p * HA:(p + 1) * HA], hot[:, O_SMP + p * P:O_SMP + (p + 1) * P], rel[:, 0:HA],
                   start=True, stop=True)
            for g in range(NG):
                c = O_SMP + (NPG + g) * P
                i = mm(bk[:, NPG * HA + g * HB:NPG * HA + (g + 1) * HB], hot[:, c:c + P],
                       rel[:, HA + g * HB:HA + (g + 1) * HB], start=True, stop=True)
            done("sbias", i)
            for n in range(4):
                h0, hn = (0, HA) if n == 0 else (HA + (n - 1) * HB, HB)
                bk = take(("toev", n), 5)
                done(("toev", n), mm(bk[0:hn, 0:VLEN], rel[:, h0:h0 + hn],
                                     hot[:, O_TOE + n * VLEN:O_TOE + (n + 1) * VLEN], start=True, stop=True))

            pe.wait_ge(s_hTp, 2)
            pe.wait_ge(s_hTs, 1)
            acc = [0]

            def win_T(w, c, j):
                bk = take(("z", c), acc[0] % 2)
                acc[0] += 1
                for k in range(KC):
                    i = mm(bk[:, 0:NT], w[:, k, j * P:(j + 1) * P], hT3[:, k, :], start=(k == 0), stop=(k == KC - 1))
                done(("z", c), i)
                return i

            def win_v(w, c0, n):
                for t, (t0, tn) in enumerate(TT):
                    bk = take(("v", c0, t), acc[0] % 2)
                    acc[0] += 1
                    for k in range(KC):
                        i = mm(bk[0:tn, 0:n], hT3[:, k, t0:t0 + tn], w[:, k, 0:n], start=(k == 0), stop=(k == KC - 1))
                    done(("v", c0, t), i)
                return i

            for t in range(12):
                name = ("win", t)
                width = 512 if t < 11 else 256
                w = landed(pe, name)[:, 0:KC * width].rearrange("p (k n) -> p k n", k=KC)
                if t in V_TILES:
                    i = win_v(w, *V_TILES[t])
                for j in range(V_TILES[t][1] // P if t in V_TILES else 0, width // P):
                    i = win_T(w, 4 * t + j, j)
                last_use[name] = ("z", 4 * t + 3) if t not in (2, 6) and t < 11 else \
                    ("z", 45) if t == 11 else ("v", V_TILES[t][0], 2)
                for b in Q_AFTER.get(t, ()):
                    pe.wait_ge(s_qrep, b + 1)
                    bk = take(("qbc", b), 2 + b % 2)
                    for j in range(4):
                        i = mm(bk[:, j * P:(j + 1) * P], qrep[:, b % 2, j, :], ident, start=True, stop=True)
                    done(("qbc", b), i)
                if t == 5:
                    pe.wait_ge(s_z, 20)
                    for tt, (t0, tn) in enumerate(TT):
                        for n, (r0, rn, _) in enumerate(KT):
                            bk = take(("kt", tt, n), 2 + (tt * 3 + n) % 2)
                            for j in range(rn):
                                i = tr(bk[0:tn, j * P:(j + 1) * P], zT3[:, r0 + j, t0:t0 + tn], ident)
                            done(("kt", tt, n), i)
                    pe.wait_ge(s_prod, 1)
                    bk = take("own", 5)
                    for c in range(10):
                        mm(bk[0:NB, 2 * c:2 * c + 2], prod[:, c * NB:(c + 1) * NB], hind, start=True, stop=True)
                    done("own", mm(bk[0:NB, HALL:2 * HALL], hot[:, O_ZERO:O_ZERO + NB], rel[:, :], start=True, stop=True))
            for t in range(4, 12):
                ada(t)

            for g in range(NG):
                for b in range(NB):
                    n = NB + g * NB + b
                    pe.wait_ge(s_qrep, n + 1)
                    bk = take(("qbd", g, b), 2 + b % 2)
                    for j in range(2):
                        i = mm(bk[:, j * P:(j + 1) * P], qrep[:, b % 2, j, :], ident, start=True, stop=True)
                    done(("qbd", g, b), i)

            pe.wait_ge(s_kred, 2 * NB)
            for h in range(2):
                bk = take(("bs", h), 4 + h)
                done(("bs", h), mm(bk[0:NB, :], ones[:, 0:NB], S[:, h * 512:(h + 1) * 512], start=True, stop=True))
            pe.wait_ge(s_pen, 1)
            bk = take("pen", 4)
            done("pen", mm(bk[:, :], ones[0:NB, :], work[0:NB, 2048:2560], start=True, stop=True))
            pe.wait_ge(s_m12, 1)
            bk = take("mxT", 5)
            done("mxT", tr(bk[0:96, 0:P], m12[:, :], ident))
            pe.wait_ge(s_ownx, 1)
            bk = take("ownx", 4)
            done("ownx", mm(bk[0:96, 0:1], ownD[:, :], ones[0:NB, 0:1], start=True, stop=True))
            pe.wait_ge(s_negm, 1)
            bk = take("negm", 5)
            mm(bk[:, 0:96], ones[0:96, :], st96[0:96, 0:96], start=True, stop=True)
            done("negm", mm(bk[0:NB, 96:96 + HS], e96, st96[0:96, 96:96 + HS], start=True, stop=True))
            pe.wait_ge(s_sum, 1)
            bk = take("sum", 4)
            mm(bk[0:96, 0:1], m12[:, :], ones[:, 0:1], start=True, stop=False)
            done("sum", mm(bk[0:96, 0:1], ownD[:, :], ones[0:NB, 0:1], start=False, stop=True))
            pe.wait_ge(s_rec, 1)
            bk = take("rs", 5)
            mm(bk[0:HA, 0:NB], h96[:, 0:HA], st96[0:96, 0:NB], start=True, stop=True)
            done("rs", mm(bk[0:HB, NB:2 * NB], h96[:, HA:HS], st96[0:96, 0:NB], start=True, stop=True))

            pe.wait_ge(s_rs, 1)
            for b in range(8):
                if uses[b]:
                    pe.wait_ge(free[b], uses[b])
            vm = [work[0:HA, i * 512:(i + 1) * 512] for i in range(2)]
            pst = [work[:, 1024 + i * P:1024 + (i + 1) * P] for i in range(2)]
            pst1 = [work[0:NB, 1280 + i * HA:1280 + (i + 1) * HA] for i in range(2)]
            with pe.Fori(0, NB // 2) as i2:
                for bb in range(2):
                    pe.wait_ge(s_pst, 2 * i2 + bb + 1)
                    for hh in range(2):
                        vt = ring[:, 4 + hh, :].rearrange("p (k n) -> p k n", k=HPG)
                        pe.wait_ge(w_full[4 + hh], i2 * (32 * HPG) + (v_val0[hh] + (bb + 1) * 16 * HPG))
                        for k in range(HPG):
                            c = (hh * HPG + k) * HA
                            i = mm(bank[6 + bb][0:HA, :], pst[bb][:, c:c + HA], vt[:, k, :],
                                   start=(c == 0), stop=False)
                        i.then_inc(s_vread[hh], 1)
                    mm(bank[6 + bb][0:HA, :], pst1[bb], v[0:NB, 2, 0:AW], start=False, stop=True).then_inc(s_ov, 1)
                for bb in range(2):
                    pe.wait_ge(s_vm, 2 * i2 + bb + 1)
                    for c in range(4):
                        i = mm(bank[4 + bb][:, c:c + 1], vm[bb][:, c * P:(c + 1) * P],
                               rinv[:, bass.ds(2 * i2 + bb, 1)], start=True, stop=True)
                    i.then_inc(s_vt, 1)
            pe.wait_ge(s_oa, NB)
            vd0 = landed(pe, ("vd", 0)).rearrange("p (g b n) -> p g b n", g=2, b=NB)
            vd2 = landed(pe, ("vd", 2))[:, 0:2048].rearrange("p (b n) -> p b n", b=NB)
            for b in range(NB):
                bk = take(("od", b), 6 + b % 2)
                for g in range(NG):
                    r = vd0[:, g, b, :] if g < 2 else vd2[:, b, :]
                    mm(bk[0:HB, 0:256], Sd4[:, b, g, :], r, start=(g == 0), stop=False)
                for g in range(NG):
                    c = NB * HA + (b * NG + g) * HB
                    i = mm(bk[0:HB, 0:256], powD[:, c:c + HB], v[0:NB, 2, AW + g * 256:AW + (g + 1) * 256],
                           start=False, stop=(g == NG - 1))
                done(("od", b), i)
            last_use[("vd", 0)] = last_use[("vd", 2)] = ("od", NB - 1)
            bk = take("odT", 4)
            for b in range(NB):
                pe.wait_ge(s_vm, NB + b + 1)
                for c in range(2):
                    i = mm(bk[:, c * NB + b:c * NB + b + 1], work[0:HB, b * 256 + c * P:b * 256 + (c + 1) * P],
                           rinv[0:HB, NB + b:NB + b + 1], start=True, stop=True)
            done("odT", i)

            def scores(n):
                u = units[n]
                nk = P * (u[2] + 1)
                for gi, (qr, kr, par, _) in enumerate(heads(u)):
                    bk = take(("sc", n, gi), 4 + (n + gi) % 2)
                    done(("sc", n, gi), mm(bk[:, 0:nk], zT3[par * HD:(par + 1) * HD, qr, u[2] * P:(u[2] + 1) * P],
                                           zT3[par * HD:(par + 1) * HD, kr, 0:nk], start=True, stop=True))

            def turn_weights(n):
                u = units[n]
                nk = P * (u[2] + 1)
                pe.wait_ge(s_pn, n + 1)
                for gi in range(len(heads(u))):
                    bk = take(("pt", n, gi), 2 + (n + gi) % 2)
                    for kt in range(u[2] + 1):
                        c = gi * nk + kt * P
                        i = tr(bk[:, kt * P:(kt + 1) * P], pk[n % 2][:, c:c + P], ident)
                    done(("pt", n, gi), i)

            def values(n):
                u = units[n]
                hh = heads(u)
                pe.wait_ge(s_pT, n + 1)
                bk = take(("po", n), n % 2)
                par = u[1] % 2
                for gi, (_, _, _, vc) in enumerate(hh):
                    for kt in range(u[2] + 1):
                        i = mm(bk[par * HD:(par + 1) * HD, 0:P], v[:, kt, vc:vc + HD],
                               pT[n % 2][:, gi * SEQ + kt * P:gi * SEQ + (kt + 1) * P],
                               start=(gi == 0 and kt == 0), stop=(gi == len(hh) - 1 and kt == u[2]))
                done(("po", n), i)

            for n in range(len(units) + 2):
                if n < len(units):
                    scores(n)
                if 1 <= n <= len(units):
                    turn_weights(n - 1)
                if n >= 2:
                    values(n - 2)

            pe.wait_ge(s_po, len(units))
            wa = landed(pe, ("wpa", 0)).rearrange("p (k n) -> p k n", k=4)
            wb = landed(pe, ("wpb", 0))[:, 0:2048].rearrange("p (k n) -> p k n", k=2)
            for j in range(KC):
                bk = take(("ya", j), j % 2)
                for k in range(4):
                    i = mm(bk[:, 0:NT], wa[:, k, j * P:(j + 1) * P], oT3[:, k, :], start=(k == 0), stop=(k == 3))
                done(("ya", j), i)
                bk = take(("yb", j), 2 + j % 2)
                for k in range(2):
                    i = mm(bk[:, 0:NT], wb[:, k, j * P:(j + 1) * P], oT3[:, 4 + k, :], start=(k == 0), stop=(k == 1))
                done(("yb", j), i)
            last_use[("wpa", 0)] = last_use[("wpb", 0)] = ("yb", KC - 1)
            pe.wait_ge(s_u, KC)
            for j in range(KC):
                half = ("wo", j // 4)
                w = landed(pe, half).rearrange("p (k n) -> p k n", k=KC)
                bk = take(("mix", j), j % 2)
                for k in range(KC):
                    i = mm(bk[:, 0:NT], w[:, k, (j % 4) * P:(j % 4 + 1) * P], hT3[:, k, :],
                           start=(k == 0), stop=(k == KC - 1))
                done(("mix", j), i)
                last_use[half] = ("mix", j)
            pe.wait_ge(s_mix, KC)
            for t, (t0, tn) in enumerate(TT):
                for h in range(2):
                    bk = take(("mt", t, h), 2 + h)
                    for j in range(4):
                        i = tr(bk[0:tn, j * P:(j + 1) * P], mixT[:, 4 * h + j, t0:t0 + tn], ident)
                    done(("mt", t, h), i)

            for h in range(2):
                pe.wait_ge(s_g2, h + 1)
                bk = take(("g2", h), 6)
                for j in range(4):
                    i = mm(bk[:, j * P:(j + 1) * P], qrep[:, h, j, :], ident, start=True, stop=True)
                done(("g2", h), i)
                bk = take(("g2s", h), 7)
                for j in range(4):
                    i = tr(bk[0:NB, j * P:(j + 1) * P], mod[:, 40 + 4 * h + j, 0:NB], ident)
                done(("g2s", h), i)
            for t, (t0, tn) in enumerate(TT):
                pe.wait_ge(s_n2, t + 1)
                for h in range(2):
                    bk = take(("nT", t, h), 4 + h)
                    for j in range(4):
                        k = 4 * h + j
                        i = tr(bk[:, j * P:j * P + tn], h2[0:tn, t, k * P:(k + 1) * P], ident[0:tn, 0:tn])
                    done(("nT", t, h), i)
            pe.wait_ge(s_wr, 5 * 16)
            pe.wait_ge(s_h2T, 3)
            bk = take("lg", 2)
            wr = work[:, 2700:2700 + KC * 36].rearrange("p (k n) -> p k n", k=KC)
            for t, (t0, tn) in enumerate(TT):
                for k in range(KC):
                    i = mm(bk[0:tn, t * 36:(t + 1) * 36], hT3[:, k, t0:t0 + tn], wr[:, k, :],
                           start=(k == 0), stop=(k == KC - 1))
            done("lg", i)
            for t, (t0, tn) in enumerate(TT):
                for h in range(2):
                    bk = take(("h2", t, h), h)
                    for j in range(4):
                        i = tr(bk[0:tn, j * P:(j + 1) * P], hT3[:, 4 * h + j, t0:t0 + tn], ident)
                    done(("h2", t, h), i)
            pe.wait_ge(s_mask, 1)
            M = work[:, 0:3 * NE].rearrange("p (t e) -> p t e", t=3)
            bk = take("pos", 3)
            mm(bk[:, 0:32], tri, M[:, 0, :], start=True, stop=True)
            mm(bk[:, 32:64], ones, M[:, 0, :], start=True, stop=False)
            mm(bk[:, 32:64], tri, M[:, 1, :], start=False, stop=True)
            mm(bk[0:NB, 64:96], ones[:, 0:NB], M[:, 0, :], start=True, stop=False)
            mm(bk[0:NB, 64:96], ones[:, 0:NB], M[:, 1, :], start=False, stop=False)
            mm(bk[0:NB, 64:96], tri[0:NB, 0:NB], M[0:NB, 2, :], start=False, stop=True)
            mm(bk[0:1, 96:128], ones[:, 0:1], M[:, 0, :], start=True, stop=False)
            mm(bk[0:1, 96:128], ones[:, 0:1], M[:, 1, :], start=False, stop=False)
            done("pos", mm(bk[0:1, 96:128], ones[0:NB, 0:1], M[0:NB, 2, :], start=False, stop=True))

            for b in range(8):
                pe.wait_ge(free[b], uses[b])

            def gather(s, nth):
                pe.wait_ge(s_G, nth)
                for k in range(KC):
                    for t, (t0, tn) in enumerate(TT):
                        i = mm(bank[s][:, k * SLOT:(k + 1) * SLOT], h2[0:tn, t, k * P:(k + 1) * P],
                               G[s][0:tn, t, :], start=(t == 0), stop=(t == 2))
                for t, (t0, tn) in enumerate(TT):
                    i = mm(bank[4 + s][0:SLOT, 0:1], G[s][0:tn, t, :], rowf[0:tn, s, t:t + 1], start=(t == 0), stop=(t == 2))
                i.then_inc(s_xg, 1)

            def gate_up(s, nth, load):
                pe.wait_ge(s_xT, nth)
                for m in range(2):
                    w = ring[:, 3 * s + m, :].rearrange("p (k n) -> p k n", k=KC)
                    pe.wait_ge(ew_full[3 * s + m], load)
                    for f in range(FC):
                        for k in range(KC):
                            i = mm(bank[2 + s][:, m * 256 + f * SLOT:m * 256 + (f + 1) * SLOT],
                                   w[:, k, f * P:(f + 1) * P], xT[s][:, k, :], start=(k == 0), stop=(k == KC - 1))
                i.then_inc(s_gu, 1)

            def down(s, nth, load):
                w = ring[:, 3 * s + 2, :].rearrange("p (f n) -> p f n", f=FC)
                pe.wait_ge(ew_full[3 * s + 2], load)
                pe.wait_ge(s_act, nth)
                for k in range(KC):
                    for f in range(FC):
                        i = mm(bank[4 + s][:, k * SLOT:(k + 1) * SLOT], w[:, f, k * P:(k + 1) * P],
                               aT[s][:, f * SLOT:(f + 1) * SLOT], start=(f == 0), stop=(f == FC - 1))
                i.then_inc(s_yt, 1)

            def rows(s, nth, before=None):
                pe.wait_ge(s_cst, 16)
                pe.wait_ge(s_yT, nth)
                if before is not None:
                    pe.wait_ge(s_yrow, before)
                for k in range(KC):
                    i = tr(bank[6 + k // 4][0:SLOT, (k % 4) * P:(k % 4 + 1) * P], yT[s][:, k, :], ident)
                i.then_inc(s_yb, 1)

            pe.wait_ge(s_round, 2)
            n_r = pe.value_load(rounds_i[0:1, 0:1], min_val=1, max_val=MAXR)
            gather(0, 1)
            with pe.Fori(0, n_r * (NE // 2)) as i2:
                gate_up(0, 2 * i2 + 1, 16 * i2 + 16)
                gather(1, 2 * i2 + 2)
                down(0, 2 * i2 + 1, 16 * i2 + 16)
                gate_up(1, 2 * i2 + 2, 16 * i2 + 16)
                rows(0, 2 * i2 + 1)
                gather(0, 2 * i2 + 3)
                down(1, 2 * i2 + 2, 16 * i2 + 16)
                rows(1, 2 * i2 + 2, 2 * i2 + 1)
                pe.wait_ge(s_yrow, 2 * i2 + 2)

        @block.scalar
        def _(act):
            A = nc.scalar.activation

            def copy(out, in_):
                return A(out, in_, ACT.Copy)

            def freed(key, ins, also=None):
                b, n = turn[key]
                ins.then_inc(free[b], 1)
                if also is not None:
                    act.wait_ge(free[b], n + 1)
                    act.sem_inc(also, 1)

            act.wait_ge(s_c, 32)
            A(crow, crow, ACT.Silu).then_inc(s_silu, 1)
            bk = filled(act, "cT")
            i = copy(cT[:, :], bk[:, 0:72])
            freed("cT", i, s_cT)
            bk = filled(act, "bT")
            i = copy(bT[:, :], bk[:, 0:48])
            freed("bT", i, s_bt)

            def root(n):
                act.wait_ge(s_var, n)
                A(sdev[:, :], sdev[:, :], ACT.Sqrt).then_inc(s_sd, 1)

            root(1)

            def ada(t):
                bk = filled(act, ("ada", t))
                if t == 0:
                    act.wait_ge(s_bT, 1)
                for j in range(4):
                    i = A(mod[:, 4 * t + j, :], bk[:, j * 9:(j + 1) * 9], ACT.Identity, bias=bT[:, 4 * t + j:4 * t + j + 1])
                freed(("ada", t), i, s_mod)

            for t in range(4):
                ada(t)
            act.wait_ge(s_mod, 4)
            for t in range(2):
                for h in range(2):
                    bk = filled(act, ("xT", t, h))
                    for j in range(4):
                        k = 4 * h + j
                        i = A(hT3[:, k, t * P:(t + 1) * P], bk[:, j * P:(j + 1) * P], ACT.Identity,
                              bias=mod[:, k, NB:NB + 1], scale=mod[:, 8 + k, NB:NB + 1])
                    freed(("xT", t, h), i, s_hTp if h else None)
            hs3 = hs[:, :].rearrange("p (k n) -> p k n", k=KC)
            for h in range(2):
                bk = filled(act, ("xT", 2, h))
                i = copy(hs3[:, 4 * h:4 * h + 4, :], bk[:, :].rearrange("p (k n) -> p k n", k=4)[:, :, 0:NB])
                freed(("xT", 2, h), i, s_hs if h else None)
            bk = filled(act, "sbias")
            i = copy(sbias[:, :], bk[:, 0:NPG * HA + NG * HB])
            freed("sbias", i, s_sbias)
            for n in range(4):
                hn = HA if n == 0 else HB
                bk = filled(act, ("toev", n))
                i = copy(toev[0:hn, n, :], bk[0:hn, 0:VLEN])
                freed(("toev", n), i, s_toev)

            def spread(n, r0, rn, b):
                if n >= 2:
                    act.wait_ge(full[turn[prev[n - 2]][0]], turn[prev[n - 2]][1] + 1)
                i = copy(qrep[:, n % 2, 0:rn, :], zT3[:, r0:r0 + rn, SEQ + b:SEQ + b + 1].to_broadcast([P, rn, P]))
                i.then_inc(s_qrep, 1)

            prev = [("qbc", b) for b in range(NB)] + [("qbd", g, b) for g in range(NG) for b in range(NB)]

            def state_copies(t):
                if t < NB:
                    jobs = [(2, t)]
                elif t == NB:
                    jobs = [(1, b) for b in range(NB)]
                else:
                    jobs = [(0, b) for b in range(NB)]
                for g, b in jobs:
                    n = (P * DIL[g] - 1) // 16
                    src = states[g][0, b].rearrange("w a h d -> (w a h d)")
                    dst = st_out[g][0, b].rearrange("w a h d -> (w a h d)")
                    m = 16 * n * 512
                    act.dma_start(dst[0:m].rearrange("(a m) -> a m", a=16),
                                  src[512:512 + m].rearrange("(a m) -> a m", a=16)).then_inc(s_st, 16)
                if t >= NB:
                    for g in ((1,) if t == NB else (0, 2)):
                        w = P * DIL[g]
                        n = (w - 1) // 16 * 16
                        act.dma_start(st_out[g][0, :, n:w - 1].rearrange("b w a h d -> b (w a h d)"),
                                      states[g][0, :, n + 1:w].rearrange("b w a h d -> b (w a h d)")).then_inc(s_st, 16)

            for t in range(12):
                width = 512 if t < 11 else 256
                j0 = 0
                if t in V_TILES:
                    c0, cn = V_TILES[t]
                    j0 = cn // P
                    for tt, (t0, tn) in enumerate(TT):
                        bk = filled(act, ("v", c0, tt))
                        i = copy(v[0:tn, tt, c0:c0 + cn], bk[0:tn, 0:cn])
                        freed(("v", c0, tt), i, s_vrow)
                for j in range(j0, width // P):
                    c = 4 * t + j
                    bk = filled(act, ("z", c))
                    if c in ZROW:
                        freed(("z", c), copy(zT3[:, ZROW[c], :], bk[:, 0:NT]), s_z)
                    else:
                        freed(("z", c), A(gates3[:, c - GA, :], bk[:, 0:NT], ACT.Sigmoid))
                for b in Q_AFTER.get(t, ()):
                    if b == 0:
                        act.wait_ge(s_z, 4)
                    spread(b, ZROW[QA], 4, b)
                    bk = filled(act, ("qbc", b))
                    if b >= 4:
                        act.wait_ge(s_kred, 2 * (b - 3))
                    i = A(qbc[:, (b % 4) * AW:(b % 4 + 1) * AW], bk[:, :], ACT.Copy, scale=QSCALE)
                    freed(("qbc", b), i, s_qbc)
                if t == 5:
                    for tt, (t0, tn) in enumerate(TT):
                        st = kst[tt % 2]
                        if tt == 0:
                            act.wait_ge(s_toes, 64)
                        if tt == 2:
                            act.wait_ge(s_kout[0], 4 * 16)
                        for n, (_, rn, c0) in enumerate(KT):
                            bk = filled(act, ("kt", tt, n))
                            i = copy(st[0:tn, c0:c0 + rn * P], bk[0:tn, 0:rn * P])
                            freed(("kt", tt, n), i, s_kst)
                        act.wait_ge(s_kst, 3 * (tt + 1))
                        ks = s_kout[tt % 2]
                        if tt < 2:
                            act.dma_start(k_prompt[0, 0, t0:t0 + tn].rearrange("s h d -> s (h d)"), st[0:tn, 0:AW]).then_inc(ks, 16)
                            for g in range(NG):
                                if g == 0 and tt == 0:
                                    continue
                                r0 = 0 if g == 0 else t0
                                act.dma_start(st_p[g][0, 0, r0:r0 + tn, 0].rearrange("s h d -> s (h d)"),
                                              st[0:tn, AW + g * 256:AW + (g + 1) * 256]).then_inc(ks, 16)
                            if tt == 0:
                                act.dma_start(v_prompt[0, 0, 0:P].rearrange("s h d -> s (h d)"), v[:, 0, 0:AW]).then_inc(ks, 16)
                        else:
                            act.dma_start(k_sample[0, :, 0].rearrange("s h d -> s (h d)"), st[0:tn, 0:AW]).then_inc(ks, 16)
                            for g in range(NG):
                                act.dma_start(st_out[g][0, :, P * DIL[g] - 1, 0].rearrange("s h d -> s (h d)"),
                                              st[0:tn, AW + g * 256:AW + (g + 1) * 256]).then_inc(ks, 16)
                    bk = filled(act, "own")
                    i = copy(own[:, 0:2 * HALL], bk[0:NB, 0:2 * HALL])
                    freed("own", i, s_own)
                if 2 <= t:
                    state_copies(t - 2)
            act.wait_ge(s_vrow, 9)
            act.dma_start(v_prompt[0, 0, P:SEQ].rearrange("s h d -> s (h d)"), v[:, 1, 0:AW]).then_inc(s_vout, 16)
            act.dma_start(v_sample[0, :, 0].rearrange("s h d -> s (h d)"), v[0:NB, 2, 0:AW]).then_inc(s_vout, 16)
            for g in range(NG):
                c = AW + g * 256
                if g:
                    act.dma_start(st_p[g][0, 0, 0:P, 1].rearrange("s h d -> s (h d)"), v[:, 0, c:c + 256]).then_inc(s_vout, 16)
                r0 = 0 if g == 0 else P
                act.dma_start(st_p[g][0, 0, r0:r0 + P, 1].rearrange("s h d -> s (h d)"), v[:, 1, c:c + 256]).then_inc(s_vout, 16)
                act.dma_start(st_out[g][0, :, P * DIL[g] - 1, 1].rearrange("s h d -> s (h d)"), v[0:NB, 2, c:c + 256]).then_inc(s_vout, 16)
            for t in range(4, 12):
                ada(t)
            for g in range(NG):
                for b in range(NB):
                    n = NB + g * NB + b
                    spread(n, ZROW[QB] + 2 * g, 2, b)
                    bk = filled(act, ("qbd", g, b))
                    if b == 0:
                        act.wait_ge(s_kred, 2 * NB) if g == 0 else act.wait_ge(s_kdred, g)
                    i = A(qbc[:, b * 256:(b + 1) * 256], bk[:, 0:256], ACT.Copy, scale=QSCALE)
                    freed(("qbd", g, b), i, s_qbc)

            act.wait_ge(s_sub, 1)
            A(S[:, :], S[:, :], ACT.Exp).then_inc(s_exp, 1)
            A(Sd[:, :], Sd[:, :], ACT.Exp).then_inc(s_exp, 1)
            A(own[:, 40:60], own[:, 40:60], ACT.Exp).then_inc(s_exp, 1)
            act.wait_ge(s_rs, 1)
            pst = [work[:, 1024 + i * P:1024 + (i + 1) * P] for i in range(2)]
            pst1 = [work[0:NB, 1280 + i * HA:1280 + (i + 1) * HA] for i in range(2)]

            def stage(bb, b):
                act.copy(pst[bb], S[:, bass.ds(b * (NPG * HA), NPG * HA)])
                act.copy(pst1[bb], powD[:, bass.ds(b * HA, HA)]).then_inc(s_pst, 1)

            for bb in range(2):
                stage(bb, bb)
            with act.Fori(0, NB // 2 - 1) as i2:
                for bb in range(2):
                    act.wait_ge(s_ov, 2 * i2 + bb + 1)
                    stage(bb, 2 * i2 + bb + 2)

            for n in range(len(units) + 1):
                if n < len(units):
                    u = units[n]
                    w = len(heads(u)) * P * (u[2] + 1)
                    act.wait_ge(s_lg, n + 1)
                    A(pk[n % 2][:, 0:w], pk[n % 2][:, 0:w], ACT.Exp, bias=stat[:, n % 2:n % 2 + 1],
                      accum_out=stat[:, 2 + n % 2:3 + n % 2]).then_inc(s_pexp, 1)
                if n >= 1:
                    m = n - 1
                    u = units[m]
                    nk = P * (u[2] + 1)
                    if m >= 2:
                        act.wait_ge(s_po, m - 1)
                    for gi in range(len(heads(u))):
                        bk = filled(act, ("pt", m, gi))
                        i = copy(pT[m % 2][:, gi * SEQ:gi * SEQ + nk], bk[:, 0:nk])
                        freed(("pt", m, gi), i, s_pT if gi == len(heads(u)) - 1 else None)

            for h in range(2):
                i = copy(qrep[:, h, :, :], mod[:, 40 + 4 * h:44 + 4 * h, NB:NB + 1].to_broadcast([P, 4, P]))
                i.then_inc(s_g2, 1)
            act.wait_ge(s_x1, 6)
            for h in range(2):
                bk = filled(act, ("g2", h))
                i = copy(g2p[:, h * 512:(h + 1) * 512], bk[:, :])
                freed(("g2", h), i, s_g2)
                bk = filled(act, ("g2s", h))
                i = copy(g2s[:, h * 512:(h + 1) * 512], bk[0:NB, :])
                freed(("g2s", h), i, s_g2)

            root(2)
            root(3)
            for t in range(2):
                for h in range(2):
                    bk = filled(act, ("nT", t, h))
                    for j in range(4):
                        k = 4 * h + j
                        i = A(hT3[:, k, t * P:(t + 1) * P], bk[:, j * P:(j + 1) * P], ACT.Identity,
                              bias=mod[:, 24 + k, NB:NB + 1], scale=mod[:, 32 + k, NB:NB + 1])
                    freed(("nT", t, h), i, s_h2T if h else None)
            for t, (t0, tn) in enumerate(TT):
                for h in range(2):
                    bk = filled(act, ("h2", t, h))
                    i = copy(h2[0:tn, t, h * 512:(h + 1) * 512], bk[0:tn, :])
                    freed(("h2", t, h), i, s_h2)
            act.wait_ge(s_rlg, 1)
            A(work[:, 400:412], work[:, 400:412], ACT.Exp).then_inc(s_rexp, 1)
            act.wait_ge(s_rlg, 2)
            A(work[:, 420:423], work[:, 420:423], ACT.Exp).then_inc(s_rexp, 1)

            act.wait_ge(s_round, 2)
            n_r = act.value_load(rounds_i[0:1, 0:1], min_val=1, max_val=MAXR)
            with act.Fori(0, n_r * (NE // 2)) as i2:
                for s in range(2):
                    nth = 2 * i2 + s + 1
                    act.wait_ge(s_gu, nth)
                    A(sg[s], bank[2 + s][:, 0:256], ACT.Silu).then_inc(s_sg, 1)
                    act.wait_ge(s_yt, nth)
                    copy(yT[s].rearrange("p k n -> p (k n)"), bank[4 + s][:, :]).then_inc(s_yT, 1)
                    act.wait_ge(s_yb, nth)
                    act.wait_ge(s_sc, nth + 1)
                    copy(yrow[s][:, 0:512], bank[6][0:SLOT, :])
                    copy(yrow[s][:, 512:DM], bank[7][0:SLOT, :]).then_inc(s_yrow, 1)
            root(4)
            act.wait_ge(s_st, 16 * (3 * NB + 3))
            act.wait_ge(s_vout, 16 * 10)
            act.wait_ge(s_kout[0], 16 * 8)
            act.wait_ge(s_kout[1], 16 * 4)

        @block.vector
        def _(dve):
            V = nc.vector
            link = chain(dve, s_dve)

            def freed(key, ins, also=None):
                b, n = turn[key]
                ins.then_inc(free[b], 1)
                if also is not None:
                    dve.wait_ge(free[b], n + 1)
                    dve.sem_inc(also, 1)

            def normalize(rows, signal=None):
                for t, (src, _, tn) in enumerate(rows):
                    link(V.bn_stats(stat[0:tn, 4:10], src[:, 0:512]))
                    link(V.bn_stats(stat[0:tn, 10:16], src[:, 512:DM]))
                    link(V.bn_aggr(nst[0:tn, t, :], stat[0:tn, 4:16]))
                V.tensor_scalar(sdev[:, :], nst[:, :, 1], EPS, None, ALU.add).then_inc(s_var, 1)
                norms[0] += 1
                dve.wait_ge(s_sd, norms[0])
                link(V.reciprocal(sdev[:, :], sdev[:, :]))
                for t, (src, dst, tn) in enumerate(rows):
                    i = V.tensor_scalar(dst, src, nst[0:tn, t, 0:1], sdev[0:tn, t:t + 1], ALU.subtract, ALU.mult)
                    if signal is None:
                        link(i)
                    else:
                        i.then_inc(signal, 1)

            norms = [0]
            link(V.memset(nst[:, :, :], 1.0))
            dve.wait_ge(s_x, 48)
            normalize([(x[0:tn, t, :], x[0:tn, t, :], tn) for t, (t0, tn) in enumerate(TT)], s_norm)

            dve.wait_ge(s_cst, 16)
            with dve.Fori(0, NB // 4) as i2:
                for bb in range(4):
                    dve.wait_ge(s_qbc, 4 * i2 + bb + 1)
                    for hh in range(2):
                        kt = ring[:, 4 + hh, :]
                        n = 8 * i2 + 2 * bb + hh
                        dve.wait_ge(w_full[4 + hh], i2 * (4 * 16 * HPG) + (bb + 1) * 16 * HPG)
                        k3 = kt.rearrange("p (k n) -> p k n", k=HPG)
                        V.tensor_tensor(k3, k3, qbc[:, bb * AW:(bb + 1) * AW].unsqueeze(1).to_broadcast([P, HPG, AW]),
                                        ALU.mult).then_inc(s_kmul, 1)
                        dve.wait_ge(s_kmul, n + 1)
                        V.tensor_reduce(S[:, bass.ds(n * (HPG * HA), HPG * HA)],
                                        kt.rearrange("p (m d) -> p m d", d=HD), AX.X, ALU.add).then_inc(s_kred, 1)
            for g in range(NG):
                kt = landed(dve, ("kd", g))[:, 0:2048]
                dve.wait_ge(s_qbc, NB + (g + 1) * NB)
                V.tensor_tensor(kt, kt, qbc[:, 0:2048], ALU.mult).then_inc(s_kdmul, 1)
                dve.wait_ge(s_kdmul, g + 1)
                i = V.tensor_reduce(Sd4[:, :, g, :], kt.rearrange("p (b h d) -> p b h d", b=NB, h=HB), AX.X, ALU.add)
                i.then_inc(s_kdred, 1)

            bsm = work[0:NB, 0:1024]
            i8 = ident[0:NB, 0:NB]
            dve.wait_ge(s_kout[0], 8 * 16)
            dve.wait_ge(s_kout[1], 4 * 16)
            for h in range(2):
                bk = filled(dve, ("bs", h))
                i = V.tensor_tensor(bsm[:, h * 512:(h + 1) * 512].rearrange("p (b n) -> p b n", b=4),
                                    bk[0:NB, :].rearrange("p (b n) -> p b n", b=4),
                                    i8[:, 4 * h:4 * h + 4].unsqueeze(2).to_broadcast([NB, 4, P]), ALU.mult)
                freed(("bs", h), i)
            dve.wait_ge(free[4], turn[("bs", 0)][1] + 1)
            dve.wait_ge(free[5], turn[("bs", 1)][1] + 1)
            pgs = work[0:NB, 1024:1152]
            link(V.tensor_reduce(pgs, bsm.rearrange("p (b n) -> p n b", b=NB), AX.X, ALU.add))
            bs = work[0:NB, 1152:1216]
            link(V.tensor_reduce(bs.rearrange("p (k h) -> p k h", k=NBLK),
                                 pgs.rearrange("p (k t h) -> p k h t", k=NBLK, t=2), AX.X, ALU.add))
            bsh = bs.rearrange("p (k h) -> p h k", k=NBLK)
            gt = work[0:NB, 1216:1728].rearrange("p (h i j) -> p h i j", h=HA, i=NBLK)
            eq = work[0:NB, 0:512].rearrange("p (h i j) -> p h i j", h=HA, i=NBLK)
            sj = bsh.unsqueeze(2).to_broadcast([NB, HA, NBLK, NBLK])
            si = bsh.unsqueeze(3).to_broadcast([NB, HA, NBLK, NBLK])
            link(V.tensor_tensor(gt, sj, si, ALU.is_gt))
            link(V.tensor_tensor(eq, sj, si, ALU.is_equal))
            tie8 = tie[0:NB, :].unsqueeze(1).to_broadcast([NB, HA, 64])
            link(V.tensor_tensor(eq.rearrange("p h i j -> p h (i j)"), eq.rearrange("p h i j -> p h (i j)"), tie8, ALU.mult))
            link(V.tensor_tensor(gt.rearrange("p h i j -> p (h i j)"), gt.rearrange("p h i j -> p (h i j)"),
                                 eq.rearrange("p h i j -> p (h i j)"), ALU.add))
            rank = work[0:NB, 512:576]
            link(V.tensor_reduce(rank.rearrange("p (h k) -> p h k", h=HA), gt, AX.X, ALU.add))
            pen = work[0:NB, 576:640]
            link(V.tensor_scalar(pen.rearrange("p (k h) -> p h k", k=NBLK), rank.rearrange("p (h k) -> p h k", h=HA),
                                 TOPK - 0.5, NEG, ALU.is_gt, ALU.mult))
            penD = work[0:NB, 2048:2560].rearrange("p (b n) -> p b n", b=NB)
            i8b = i8.unsqueeze(2).to_broadcast([NB, NB, 64])
            V.tensor_tensor(penD, i8b, pen.unsqueeze(1).to_broadcast([NB, NB, 64]), ALU.mult).then_inc(s_pen, 1)

            dve.wait_ge(s_sbias, 1)
            S3 = S[:, :].rearrange("p (b n) -> p b n", b=NB)
            link(V.tensor_tensor(S3, S3, sbias[:, 0:P].unsqueeze(1).to_broadcast([P, NB, P]), ALU.add))
            Sd3 = Sd[:, :].rearrange("p (b n) -> p b n", b=NB)
            link(V.tensor_tensor(Sd3, Sd3, sbias[:, P:P + NG * HB].unsqueeze(1).to_broadcast([P, NB, NG * HB]), ALU.add))
            bk = filled(dve, "pen")
            Sb = S[:, :].rearrange("p (q t h) -> p q t h", t=2, h=HA)
            i = V.tensor_tensor(Sb, Sb, bk[:, :].rearrange("p (q h) -> p q h", h=HA).unsqueeze(2).to_broadcast([P, NB * NBLK, 2, HA]), ALU.add)
            freed("pen", i)
            dve.wait_ge(free[4], turn["pen"][1] + 1)
            m3 = m12[:, :].rearrange("p (b h) -> p b h", b=NB)
            link(V.tensor_reduce(m3[:, :, 0:HA], S4.rearrange("p b k h -> p b h k"), AX.X, ALU.max))
            V.tensor_reduce(m3[:, :, HA:HS], Sd4.rearrange("p b g h -> p b h g"), AX.X, ALU.max).then_inc(s_m12, 1)
            dve.wait_ge(s_own, 1)
            ownl = own[:, 40:60]
            link(V.tensor_scalar(own[:, 0:HALL], own[:, 0:HALL], QSCALE, None, ALU.mult))
            link(V.tensor_tensor(ownl, own[:, 0:HALL], own[:, HALL:2 * HALL], ALU.add))
            o12 = own[:, 0:HS]
            link(V.tensor_copy(o12[:, 0:HA], ownl[:, 0:HA]))
            link(V.tensor_reduce(o12[:, HA:HS], ownl[:, HA:HALL].rearrange("p (g h) -> p h g", g=NG), AX.X, ALU.max))
            i8c = i8.unsqueeze(2).to_broadcast([NB, NB, HS])
            ownD3 = ownD[:, :].rearrange("p (b h) -> p b h", b=NB)
            V.tensor_tensor(ownD3, i8c, o12.unsqueeze(1).to_broadcast([NB, NB, HS]), ALU.mult).then_inc(s_ownx, 1)
            bk = filled(dve, "mxT")
            mrow = st96[0:96, 110:111]
            i = V.tensor_reduce(mrow, bk[0:96, 0:P], AX.X, ALU.max)
            freed("mxT", i)
            dve.wait_ge(free[5], turn["mxT"][1] + 1)
            bk = filled(dve, "ownx")
            i = V.tensor_tensor(mrow, mrow, bk[0:96, 0:1], ALU.max)
            freed("ownx", i)
            dve.wait_ge(free[4], turn["ownx"][1] + 1)
            link(V.tensor_scalar(mrow, mrow, -1.0, None, ALU.mult))
            link(V.tensor_scalar(st96[0:96, 0:96], ident[0:96, 0:96], mrow, None, ALU.mult))
            V.tensor_scalar(st96[0:96, 96:96 + HS], h96, mrow, None, ALU.mult).then_inc(s_negm, 1)
            bk = filled(dve, "negm")
            nm = bk[:, 0:96].rearrange("p (b h) -> p b h", b=NB)
            V.tensor_tensor(S4, S4, nm[:, :, 0:HA].unsqueeze(2).to_broadcast([P, NB, NPG, HA]), ALU.add)
            V.tensor_tensor(Sd4, Sd4, nm[:, :, HA:HS].unsqueeze(2).to_broadcast([P, NB, NG, HB]), ALU.add)
            V.tensor_tensor(ownl[:, 0:HA], ownl[:, 0:HA], bk[0:NB, 96:96 + HA], ALU.add)
            i = V.tensor_tensor(ownl[:, HA:HALL].rearrange("p (g h) -> p g h", g=NG),
                                ownl[:, HA:HALL].rearrange("p (g h) -> p g h", g=NG),
                                bk[0:NB, 96 + HA:96 + HS].unsqueeze(1).to_broadcast([NB, NG, HB]), ALU.add)
            freed("negm", i, s_sub)
            dve.wait_ge(s_exp, 3)
            link(V.tensor_reduce(m3[:, :, 0:HA], S4.rearrange("p b k h -> p b h k"), AX.X, ALU.add))
            link(V.tensor_reduce(m3[:, :, HA:HS], Sd4.rearrange("p b g h -> p b h g"), AX.X, ALU.add))
            link(V.tensor_copy(o12[:, 0:HA], ownl[:, 0:HA]))
            link(V.tensor_reduce(o12[:, HA:HS], ownl[:, HA:HALL].rearrange("p (g h) -> p h g", g=NG), AX.X, ALU.add))
            V.tensor_tensor(ownD3, i8c, o12.unsqueeze(1).to_broadcast([NB, NB, HS]), ALU.mult).then_inc(s_sum, 1)
            V.tensor_tensor(powD[:, 0:NB * HA].rearrange("p (b h) -> p b h", b=NB), i8.unsqueeze(2).to_broadcast([NB, NB, HA]),
                            ownl[:, 0:HA].unsqueeze(1).to_broadcast([NB, NB, HA]), ALU.mult)
            link(V.tensor_tensor(powD[:, NB * HA:].rearrange("p (b h) -> p b h", b=NB), i8c,
                                 ownl[:, HA:HALL].unsqueeze(1).to_broadcast([NB, NB, NG * HB]), ALU.mult))
            bk = filled(dve, "sum")
            i = V.reciprocal(mrow, bk[0:96, 0:1])
            freed("sum", i)
            dve.wait_ge(free[4], turn["sum"][1] + 1)
            V.tensor_scalar(st96[0:96, 0:NB], e96, mrow, None, ALU.mult).then_inc(s_rec, 1)
            bk = filled(dve, "rs")
            V.tensor_copy(rinv[:, 0:NB], bk[0:NB, 0:NB])
            i = V.tensor_copy(rinv[0:HB, NB:2 * NB], bk[0:HB, NB:2 * NB])
            freed("rs", i, s_rs)

            vm = [work[0:HA, i * 512:(i + 1) * 512] for i in range(2)]
            with dve.Fori(0, NB // 2) as i2:
                for bb in range(2):
                    dve.wait_ge(s_ov, 2 * i2 + bb + 1)
                    V.tensor_tensor(vm[bb], bank[6 + bb][0:HA, :], blkdiag[0:HA, :], ALU.mult).then_inc(s_vm, 1)
                for bb in range(2):
                    dve.wait_ge(s_vt, 2 * i2 + bb + 1)
                    V.tensor_copy(oT3[:, 0:4, bass.ds(2 * i2 + (SEQ + bb), 1)],
                                  bank[4 + bb][:, 0:4].unsqueeze(2)).then_inc(s_oa, 1)
            for b in range(NB):
                bk = filled(dve, ("od", b))
                i = V.tensor_tensor(work[0:HB, b * 256:(b + 1) * 256], bk[0:HB, 0:256], blkdiag[0:HB, 0:256], ALU.mult)
                freed(("od", b), i, s_vm)
            bk = filled(dve, "odT")
            i = V.tensor_copy(oT3[:, 4:6, SEQ:NT], bk[:, 0:2 * NB].rearrange("p (c b) -> p c b", c=2))
            freed("odT", i)

            def logits(n):
                u = units[n]
                nk = P * (u[2] + 1)
                if n >= 2:
                    dve.wait_ge(s_pT, n - 1)
                if n == 0:
                    dve.wait_ge(s_toea, 16)
                if u[0] == "b" and n == 2 * HA:
                    dve.wait_ge(s_toeb, 16)
                hh = heads(u)
                for gi in range(len(hh)):
                    row = toe_a[:, u[1], nk - 1:nk] if u[0] == "a" else toe_b[:, gi * HB + u[1], nk - 1:nk]
                    bias = bass.AP(row.tensor, row.offset, [list(row.ap[0]), [-1, nk]])
                    bk = filled(dve, ("sc", n, gi))
                    i = V.scalar_tensor_tensor(pk[n % 2][:, gi * nk:(gi + 1) * nk], bk[:, 0:nk], QSCALE, bias,
                                               ALU.mult, ALU.add)
                    freed(("sc", n, gi), i)
                b, nt = turn[("sc", n, len(hh) - 1)]
                dve.wait_ge(free[b], nt + 1)
                V.tensor_reduce(stat[:, n % 2:n % 2 + 1], pk[n % 2][:, 0:len(hh) * nk], AX.X, ALU.max, negate=True).then_inc(s_lg, 1)

            def norm(n):
                u = units[n]
                w = len(heads(u)) * P * (u[2] + 1)
                dve.wait_ge(s_pexp, n + 1)
                r = stat[:, 20 + n % 2:21 + n % 2]
                link(V.reciprocal(r, stat[:, 2 + n % 2:3 + n % 2]))
                V.tensor_scalar(pk[n % 2][:, 0:w], pk[n % 2][:, 0:w], r, None, ALU.mult).then_inc(s_pn, 1)

            def output(n):
                u = units[n]
                par = u[1] % 2
                row = (0 if u[0] == "a" else 4) + u[1] // 2
                bk = filled(dve, ("po", n))
                i = V.tensor_copy(oT3[par * HD:(par + 1) * HD, row, u[2] * P:(u[2] + 1) * P], bk[par * HD:(par + 1) * HD, 0:P])
                freed(("po", n), i, s_po)

            for n in range(len(units) + 3):
                if n < len(units):
                    logits(n)
                if 1 <= n <= len(units):
                    norm(n - 1)
                if n >= 3:
                    output(n - 3)

            t1, t2 = work[:, 0:NT], work[:, 512:512 + NT]
            for j in range(KC):
                bk = filled(dve, ("ya", j))
                i = V.tensor_tensor(t1, bk[:, 0:NT], gates3[:, j, :], ALU.mult)
                freed(("ya", j), i)
                bk = filled(dve, ("yb", j))
                i = V.tensor_tensor(t2, bk[:, 0:NT], gates3[:, 8 + j, :], ALU.mult)
                freed(("yb", j), i)
                dve.wait_ge(free[turn[("yb", j)][0]], turn[("yb", j)][1] + 1)
                i = V.tensor_tensor(hT3[:, j, :], t1, t2, ALU.add)
                i.then_inc(s_u, 1)
                dve.wait_ge(s_u, j + 1)
            for j in range(KC):
                bk = filled(dve, ("mix", j))
                V.tensor_scalar(mixT[:, j, 0:SEQ], bk[:, 0:SEQ], mod[:, 16 + j, NB:NB + 1], None, ALU.mult)
                i = V.tensor_tensor(mixT[:, j, SEQ:NT], bk[:, SEQ:NT], mod[:, 16 + j, 0:NB], ALU.mult)
                freed(("mix", j), i, s_mix)

            dve.wait_ge(s_x2, 48)
            for t, (t0, tn) in enumerate(TT):
                for h in range(2):
                    c = slice(h * 512, (h + 1) * 512)
                    bk = filled(dve, ("mt", t, h))
                    i = V.scalar_tensor_tensor(x[0:tn, t, c], x[0:tn, t, c], ALPHA, bk[0:tn, :], ALU.mult, ALU.add)
                    freed(("mt", t, h), i, s_x1)
            dve.wait_ge(s_x1, 6)
            dve.wait_ge(s_ln1, 32)
            dve.wait_ge(s_vout, 10 * 16)
            normalize([(x[0:tn, t, :], x[0:tn, t, :], tn) for t, (t0, tn) in enumerate(TT)])
            for t, (t0, tn) in enumerate(TT):
                xt = x[0:tn, t, :]
                link(V.tensor_tensor(xt, xt, lng[0:tn, :], ALU.mult))
                link(V.tensor_tensor(xt, xt, lnb[0:tn, :], ALU.add))
            normalize([(x[0:tn, t, :], h2[0:tn, t, :], tn) for t, (t0, tn) in enumerate(TT)], s_n2)
            for h in range(2):
                bk = filled(dve, ("nT", 2, h))
                hv = hT3[:, 4 * h:4 * h + 4, SEQ:NT]
                i = V.tensor_tensor(hv, bk[:, :].rearrange("p (k n) -> p k n", k=4)[:, :, 0:NB],
                                    mod[:, 32 + 4 * h:36 + 4 * h, 0:NB], ALU.mult)
                freed(("nT", 2, h), i)
                dve.wait_ge(free[4 + h], turn[("nT", 2, h)][1] + 1)
                i = V.tensor_tensor(hv, hv, mod[:, 24 + 4 * h:28 + 4 * h, 0:NB], ALU.add)
                link(i)
            V.memset(work[:, 0:512], 0.0).then_inc(s_h2T, 1)

            lg = work[:, 112:220].rearrange("p (t n) -> p t n", t=3)
            dve.wait_ge(s_h2T, 3)
            dve.wait_ge(s_rb, 32)
            rb = work[:, 2600:2636]
            bk = filled(dve, "lg")
            link(V.tensor_tensor(lg[:, 0:2, :], bk[:, 0:72].rearrange("p (t n) -> p t n", t=2),
                                 rb.unsqueeze(1).to_broadcast([P, 2, 36]), ALU.add))
            i = V.tensor_tensor(lg[0:NB, 2, :], bk[0:NB, 72:108], rb[0:NB, :], ALU.add)
            freed("lg", i)
            dve.wait_ge(free[2], turn["lg"][1] + 1)
            lgg = lg[:, :, 0:NGRP]
            lge = lg[:, :, NGRP:36]

            def rank_of(out, s3, n, a, b):
                A_ = work[:, a:a + 3 * n * n].rearrange("p (t i j) -> p t i j", t=3, i=n)
                B_ = work[:, b:b + 3 * n * n].rearrange("p (t i j) -> p t i j", t=3, i=n)
                j_ = s3.unsqueeze(2).to_broadcast([P, 3, n, n])
                i_ = s3.unsqueeze(3).to_broadcast([P, 3, n, n])
                link(V.tensor_tensor(A_, j_, i_, ALU.is_gt))
                link(V.tensor_tensor(B_, j_, i_, ALU.is_equal))
                tt = tie.rearrange("p (i j) -> p i j", i=8)[:, 0:n, 0:n].unsqueeze(1).to_broadcast([P, 3, n, n])
                link(V.tensor_tensor(B_, B_, tt, ALU.mult))
                link(V.tensor_tensor(A_, A_, B_, ALU.add))
                link(V.tensor_reduce(out, A_, AX.X, ALU.add))

            rk4 = work[:, 230:242].rearrange("p (t n) -> p t n", t=3)
            ohg = work[:, 242:254].rearrange("p (t n) -> p t n", t=3)
            gm = work[:, 254:257]
            ex = work[:, 400:412].rearrange("p (t n) -> p t n", t=3)
            rank_of(rk4, lgg, NGRP, 600, 700)
            link(V.tensor_scalar(ohg, rk4, 0.0, None, ALU.is_equal))
            link(V.tensor_reduce(gm, lgg, AX.X, ALU.max))
            V.tensor_tensor(ex, lgg, gm.unsqueeze(2).to_broadcast([P, 3, NGRP]), ALU.subtract).then_inc(s_rlg, 1)
            les = work[:, 260:284].rearrange("p (t e) -> p t e", t=3)
            tmp4 = work[:, 800:896].rearrange("p (t e g) -> p t e g", t=3, g=NGRP)
            for t in range(3):
                link(V.tensor_tensor(tmp4[:, t], lge[:, t, :].rearrange("p (g e) -> p e g", g=NGRP),
                                     ohg[:, t, :].unsqueeze(1).to_broadcast([P, EG, NGRP]), ALU.mult))
            link(V.tensor_reduce(les, tmp4, AX.X, ALU.add))
            rk8 = work[:, 290:314].rearrange("p (t e) -> p t e", t=3)
            rank_of(rk8, les, EG, 1000, 1200)
            oh = [work[:, 320 + 24 * i:344 + 24 * i].rearrange("p (t e) -> p t e", t=3) for i in range(2)]
            vv = [work[:, 370 + 3 * i:373 + 3 * i] for i in range(2)]
            tm = work[:, 1400:1424].rearrange("p (t e) -> p t e", t=3)
            for i_ in range(2):
                link(V.tensor_scalar(oh[i_], rk8, float(i_), None, ALU.is_equal))
                link(V.tensor_tensor(tm, oh[i_], les, ALU.mult))
                link(V.tensor_reduce(vv[i_], tm, AX.X, ALU.add))
            V.tensor_tensor(work[:, 420:423], vv[1], vv[0], ALU.subtract).then_inc(s_rlg, 1)
            ohe = [work[:, 1500 + 96 * i:1596 + 96 * i].rearrange("p (t g e) -> p t g e", t=3, g=NGRP) for i in range(2)]
            for i_ in range(2):
                for t in range(3):
                    link(V.tensor_tensor(ohe[i_][:, t], ohg[:, t, :].unsqueeze(2).to_broadcast([P, NGRP, EG]),
                                         oh[i_][:, t, :].unsqueeze(1).to_broadcast([P, NGRP, EG]), ALU.mult))
            M = work[:, 0:96]
            V.tensor_tensor(M, work[:, 1500:1596], work[:, 1596:1692], ALU.add).then_inc(s_mask, 1)
            dve.wait_ge(s_rexp, 2)
            sm4, e2, den = work[:, 430:433], work[:, 420:423], work[:, 436:439]
            link(V.tensor_reduce(sm4, ex, AX.X, ALU.add))
            link(V.tensor_scalar(den, e2, 1.0, None, ALU.add))
            link(V.tensor_tensor(den, den, sm4, ALU.mult))
            link(V.reciprocal(den, den))
            link(V.tensor_copy(wts[:, :, 0], den))
            link(V.tensor_tensor(wts[:, :, 1], den, e2, ALU.mult))
            pos = work[:, 1700:1796]
            link(V.memset(pos, 0.0))
            bk = filled(dve, "pos")
            link(V.tensor_copy(pos[:, 0:64], bk[:, 0:64]))
            link(V.tensor_copy(pos[0:NB, 64:96], bk[0:NB, 64:96]))
            mc = work[0:1, 440:441]
            i = V.tensor_reduce(mc, bk[0:1, 96:128], AX.X, ALU.max)
            freed("pos", i)
            dve.wait_ge(free[3], turn["pos"][1] + 1)
            rr = work[0:1, 442:443]
            link(V.tensor_scalar(rr, mc, float(SLOT), 1.0, ALU.is_gt, ALU.add))
            for r in range(2, MAXR):
                link(V.tensor_scalar(work[0:1, 444:445], mc, float(r * SLOT), None, ALU.is_gt))
                link(V.tensor_tensor(rr, rr, work[0:1, 444:445], ALU.add))
            V.tensor_copy(rounds_i[:, :], rr).then_inc(s_round, 1)
            pm = work[:, 1800:1896]
            link(V.tensor_scalar(pm, pos, 1.0, None, ALU.add))
            link(V.tensor_tensor(pm, pm, M, ALU.mult))
            link(V.memset(posx[:, :, MAXR * NE:], -1.0))
            for r in range(MAXR):
                i = V.tensor_scalar(posx[:, :, r * NE:(r + 1) * NE], pm.rearrange("p (t e) -> p t e", t=3),
                                    -1.0 - SLOT * r, None, ALU.add)
                link(i)

            def places(s, n):
                V.tensor_copy(rowf[:, s, 0:3], rowx[:, :, bass.ds(n, 1)].rearrange("p t o -> p (t o)"))
                for t in range(3):
                    i = V.tensor_scalar(G[s][:, t, :], iota, posx[:, t, bass.ds(n, 1)], None, ALU.is_equal)
                i.then_inc(s_G, 1)

            tok = cst[:, C_TOK:C_TOK + 3]
            ohe2 = work[:, 1596:1692].rearrange("p (t e) -> p t e", t=3)
            rx = rowx[:, :, 0:NE]
            link(V.tensor_scalar(rx, ohe2, float(NT), None, ALU.mult))
            link(V.tensor_tensor(rx, rx, tok.unsqueeze(2).to_broadcast([P, 3, NE]), ALU.add))
            for r in range(1, MAXR):
                link(V.tensor_copy(rowx[:, :, r * NE:(r + 1) * NE], rx))
            link(V.memset(rowx[:, :, MAXR * NE:], 0.0))
            dve.wait_ge(s_h2, 6)
            places(0, 0)
            dve.sem_inc(s_round, 1)
            n_r = dve.value_load(rounds_i[0:1, 0:1], min_val=1, max_val=MAXR)

            def tokens(s, nth):
                dve.wait_ge(s_xg, nth)
                V.tensor_copy(xT[s].rearrange("p k n -> p (k n)"), bank[s][:, :]).then_inc(s_xT, 1)
                dve.wait_ge(s_sc, nth)
                V.tensor_scalar(stat[0:SLOT, 23:24], bank[4 + s][0:SLOT, 0:1], 0.5, 1e6, ALU.is_lt, ALU.mult).then_inc(s_big, 1)
                dve.wait_ge(s_big, nth)
                V.scalar_tensor_tensor(ridx[:, s:s + 1], bank[4 + s][0:SLOT, 0:1], -1.0, stat[0:SLOT, 23:24],
                                       ALU.add, ALU.max).then_inc(s_idx, 1)

            tokens(0, 1)
            with dve.Fori(0, n_r * (NE // 2)) as i2:
                for s in range(2):
                    n = 2 * i2 + s
                    places(1 - s, n + 1)
                    dve.wait_ge(s_sg, n + 1)
                    V.tensor_tensor(aT[s], sg[s], bank[2 + s][:, 256:512], ALU.mult).then_inc(s_act, 1)
                    tokens(1 - s, n + 2)

            dve.wait_ge(s_ln2, 32)
            dve.wait_ge(s_g2, 6)
            for t, (t0, tn) in enumerate(TT):
                ya, yb = ring[0:tn, t, 0:DM], ring[0:tn, t, DM:2 * DM]
                xt = x[0:tn, t, :]
                dve.wait_ge(s_gat, 96)
                link(V.tensor_scalar(ya, ya, wts[0:tn, t, 0:1], None, ALU.mult))
                link(V.scalar_tensor_tensor(ya, yb, wts[0:tn, t, 1:2], ya, ALU.mult, ALU.add))
                link(V.tensor_tensor(ya, ya, g2p[0:tn, :] if t < 2 else g2s, ALU.mult))
                link(V.scalar_tensor_tensor(xt, xt, ALPHA, ya, ALU.mult, ALU.add))
            normalize([(x[0:tn, t, :], x[0:tn, t, :], tn) for t, (t0, tn) in enumerate(TT)])
            for t, (t0, tn) in enumerate(TT):
                xt = x[0:tn, t, :]
                link(V.tensor_tensor(xt, xt, lng[0:tn, :], ALU.mult))
                V.tensor_tensor(xt, xt, lnb[0:tn, :], ALU.add).then_inc(s_y, 1)

        @block.gpsimd
        def _(pool):
            def load_w(name):
                at = weights.index(name)
                if at >= 4:
                    filled(pool, last_use[weights[at - 4]])
                dst = ring[:, slot_of(name), :]
                kind, t = name
                if kind == "ada":
                    src = w_ada[0].rearrange("(k p) n -> p k n", p=P)[:, :, t * 512:(t + 1) * 512]
                elif kind == "win":
                    w = 512 if t < 11 else 256
                    src = w_in[0].rearrange("(k p) n -> p k n", p=P)[:, :, t * 512:t * 512 + w]
                elif kind == "wo":
                    src = w_out[0].rearrange("(k p) n -> p k n", p=P)[:, :, t * 512:(t + 1) * 512]
                else:
                    src = (w_proj_a if kind == "wpa" else w_proj_b)[0].rearrange("(k p) n -> p k n", p=P)
                n = src.shape[1] * src.shape[2]
                pool.dma_start(dst[:, 0:n].rearrange("p (k n) -> p k n", k=src.shape[1]), src)\
                    .then_inc(w_full[slot_of(name)], 16)

            for name in weights[0:4]:
                load_w(name)
            pool.wait_ge(s_bt, 17)
            nc.gpsimd.tensor_scalar(bT[:, 8:16], bT[:, 8:16], 1.0, None, ALU.add)
            nc.gpsimd.tensor_scalar(bT[:, 32:40], bT[:, 32:40], 1.0, None, ALU.add).then_inc(s_bT, 1)
            for name in weights[4:8]:
                load_w(name)
            pool.wait_ge(s_hs, 1)
            hs3 = hs[:, :].rearrange("p (k n) -> p k n", k=KC)
            nc.gpsimd.tensor_tensor(hs3, hs3, mod[:, 8:16, 0:NB], ALU.mult).then_inc(s_pool, 1)
            pool.wait_ge(s_pool, 1)
            nc.gpsimd.tensor_tensor(hT3[:, :, SEQ:NT], hs3, mod[:, 0:8, 0:NB], ALU.add).then_inc(s_hTs, 1)
            pool.wait_ge(s_toev, 4)
            pool.dma_start(toe_d[0:HA * VLEN].rearrange("(h w) -> h w", h=HA), toev[:, 0, :]).then_inc(s_toes, 16)
            for g in range(NG):
                a = (HA + g * HB) * VLEN
                pool.dma_start(toe_d[a:a + HB * VLEN].rearrange("(h w) -> h w", h=HB), toev[0:HB, 1 + g, :]).then_inc(s_toes, 16)
            pool.wait_ge(s_toes, 64)
            pool.wait_ge(s_hTp, 2)
            pool.wait_ge(s_hs, 1)

            def toeplitz(h0, hn):
                return bass.AP(toe_d, h0 * VLEN, [[1, P], [VLEN, hn], [1, SEQ]])

            pool.dma_start(toe_b, toeplitz(HA, NG * HB)).then_inc(s_toeb, 16)
            for name in weights[8:14]:
                load_w(name)
            pool.wait_ge(s_z, 20)
            q3 = [zT3[:, 0:4, SEQ:NT], zT3[:, 8:14, SEQ:NT]]
            k3 = [zT3[:, 4:8, SEQ:NT], zT3[:, 14:20, SEQ:NT]]
            nc.gpsimd.tensor_tensor(prod[:, 0:4 * NB].rearrange("p (c b) -> p c b", c=4), q3[0], k3[0], ALU.mult)
            nc.gpsimd.tensor_tensor(prod[:, 4 * NB:].rearrange("p (c b) -> p c b", c=6), q3[1], k3[1], ALU.mult).then_inc(s_prod, 1)
            for name in weights[14:20]:
                load_w(name)
            filled(pool, ("z", 45))
            pool.dma_start(toe_a, toeplitz(0, HA)).then_inc(s_toea, 16)
            for name in weights[20:]:
                load_w(name)
            pool.wait_ge(s_po, len(units))
            pool.dma_start(x[:, 0:2, :], x_prompt[0].rearrange("(t p) d -> p t d", p=P)).then_inc(s_x2, 32)
            pool.dma_start(x[0:NB, 2, :], x_sample[:, 0, :]).then_inc(s_x2, 16)
            wr = work[:, 2700:2700 + KC * 36].rearrange("p (k n) -> p k n", k=KC)
            pool.dma_start(wr[:, :, 0:NGRP], w_rg[0].rearrange("(k p) n -> p k n", p=P)).then_inc(s_wr, 16)
            for g in range(NGRP):
                c = NGRP + g * EG
                pool.dma_start(wr[:, :, c:c + EG], w_re[0, g].rearrange("(k p) n -> p k n", p=P)).then_inc(s_wr, 16)
            pool.dma_start(work[:, 2600:2604], b_rg[0].partition_broadcast(P)).then_inc(s_rb, 16)
            pool.dma_start(work[:, 2604:2636], b_re[0].rearrange("g e -> (g e)").partition_broadcast(P)).then_inc(s_rb, 16)
            pool.dma_start(lng, ln1_g[0].partition_broadcast(P)).then_inc(s_ln1, 16)
            pool.dma_start(lnb, ln1_b[0].partition_broadcast(P)).then_inc(s_ln1, 16)
            pool.wait_ge(s_n2, 3)
            pool.dma_start(lng, ln2_g[0].partition_broadcast(P)).then_inc(s_ln2, 16)
            pool.dma_start(lnb, ln2_b[0].partition_broadcast(P)).then_inc(s_ln2, 16)
            pool.wait_ge(s_round, 2)
            n_r = pool.value_load(rounds_i[0:1, 0:1], min_val=1, max_val=MAXR)
            pool.sem_inc(s_sc, 2)
            with pool.Fori(0, n_r * (NE // 2)) as i2:
                for s in range(2):
                    nth = pool.snap(2 * i2 + s + 1)
                    pool.wait_ge(s_idx, nth)
                    pool.wait_ge(s_yrow, nth)
                    pool.sem_inc(s_scat, 1)
                    pool.indirect_dma_start(
                        out=ys_d[:, :], out_offset=bass.IndirectOffsetOnAxis(ap=ridx[:, s:s + 1], axis=0),
                        in_=yrow[s], in_offset=None, bounds_check=2 * NT - 1, oob_is_err=False,
                    ).then_inc(s_yst[s], 16)
                    pool.wait_ge(s_yst[s], 16 * i2 + 16)
                    pool.sem_inc(s_sc, 1)
            for t, (t0, tn) in enumerate(TT):
                for i_ in range(2):
                    pool.dma_start(ring[0:tn, t, i_ * DM:(i_ + 1) * DM], ys_d[i_ * NT + t0:i_ * NT + t0 + tn, :]).then_inc(s_gat, 16)

        @block.sync
        def _(sp):
            sp.dma_start(crow[0:NB, :], c_sample[:, :]).then_inc(s_c, 16)
            sp.dma_start(crow[NB:NB + 1, :], c_prompt[:, :]).then_inc(s_c, 16)
            sp.dma_start(cst[:, :], consts[:, :]).then_inc(s_cst, 16)
            sp.dma_start(brow_t, b_ada[0].rearrange("(c p) -> c p", p=P)).then_inc(s_bt, 16)
            sp.dma_start(x[:, 0:2, :], x_prompt[0].rearrange("(t p) d -> p t d", p=P)).then_inc(s_x, 32)
            sp.dma_start(x[0:NB, 2, :], x_sample[:, 0, :]).then_inc(s_x, 16)
            sp.dma_start(hot, onehots[:, :]).then_inc(s_hot, 16)
            sp.dma_start(rel[0:BUCKETS, :], rel_bias[:, :]).then_inc(s_hot, 16)
            sp.dma_start(rel[BUCKETS:BUCKETS + 1, :], negrow[:, :]).then_inc(s_hot, 16)
            sp.dma_start(pt[:, :], page_table.rearrange("(o b) n -> o (b n)", o=1)).then_inc(s_pt, 16)
            sp.wait_ge(s_pt, 16)
            n_phys = k_pages.shape[1]

            def pages(cache, b, hh):
                for k in range(HPG):
                    page = sp.value_load(pt[0:1, bass.ds(b * NPG + (hh * HPG + k), 1)], min_val=0, max_val=n_phys - 1)
                    src = cache[0, bass.ds(page, 1)].rearrange("o t h d -> (o t) (h d)")
                    sp.dma_start(ring[:, 4 + hh, k * AW:(k + 1) * AW], src).then_inc(w_full[4 + hh], 16)

            for hh in range(2):
                pages(k_pages, 0, hh)
            with sp.Fori(1, NB) as b:
                for hh in range(2):
                    sp.wait_ge(s_kred, 2 * b + (hh - 1))
                    pages(k_pages, b, hh)

            def window(g, kv, dst):
                src = states[g][0].rearrange("b (r d) a h e -> d a r b (h e)", d=DIL[g])[0, kv]
                return dst, src

            def load_window(name, g, kv, c):
                dst = ring[:, slot_of(name), c:c + 2048].rearrange("p (b n) -> p b n", b=NB)
                dst, src = window(g, kv, dst)
                sp.dma_start(dst, src).then_inc(w_full[slot_of(name)], 16)

            for g in range(NG):
                sp.wait_ge(s_kred, 2 * NB - 1 + g) if g < 2 else sp.wait_ge(s_kdred, 1)
                load_window(("kd", g), g, 0, 0)
            for hh in range(2):
                sp.wait_ge(s_kdred, 3 - hh)
                pages(v_pages, 0, hh)
            with sp.Fori(1, NB) as b:
                for hh in range(2):
                    sp.wait_ge(s_vread[hh], b)
                    pages(v_pages, b, hh)
            sp.wait_ge(s_vread[0], NB)
            load_window(("vd", 0), 0, 1, 0)
            load_window(("vd", 0), 1, 1, 2048)
            sp.wait_ge(s_vread[1], NB)
            load_window(("vd", 2), 2, 1, 0)

            def load_expert(s, m, e):
                w = (w_eg, w_eu, w_ed)[m]
                src = w[0, bass.ds(e, 1)].rearrange("o (k p) n -> p (o k) n", p=P)
                k = FC if m == 2 else KC
                sp.dma_start(ring[:, 3 * s + m, :].rearrange("p (k n) -> p k n", k=k), src).then_inc(ew_full[3 * s + m], 16)

            for slot in (4, 5, 0, 1, 2, 3):
                filled(sp, last_use[(("wpa", 0), ("wpb", 0), ("wo", 0), ("wo", 1), ("vd", 0), ("vd", 2))[slot]])
                load_expert(slot // 3, slot % 3, slot // 3)
            sp.wait_ge(s_round, 2)
            n_r = sp.value_load(rounds_i[0:1, 0:1], min_val=1, max_val=MAXR)
            with sp.Fori(0, n_r * (NE // 2) - 1) as m2:
                e = ((m2 + 1) % (NE // 2)) * 2
                for s in range(2):
                    sp.wait_ge(s_gu, 2 * m2 + s + 1)
                    load_expert(s, 0, e + s)
                    load_expert(s, 1, e + s)
                    sp.wait_ge(s_yt, 2 * m2 + s + 1)
                    load_expert(s, 2, e + s)
            for t, (t0, tn) in enumerate(TT):
                sp.wait_ge(s_y, t + 1)
                dst = y_prompt[0, t0:t0 + tn, :] if t < 2 else y_sample[:, 0, :]
                sp.dma_start(dst, x[0:tn, t, :]).then_inc(s_out, 16)
            sp.wait_ge(s_out, 48)


_INS = ["x_prompt", "x_sample", "cache_k_pages", "cache_v_pages", "page_table", "state_dil1_kv",
        "state_dil4_kv", "state_dil16_kv", "c_prompt", "c_sample", "rel_bias", "w_ada", "b_ada", "w_in",
        "w_proj_a", "w_proj_b", "w_out", "ln1_g", "ln1_b", "w_router_g", "b_router_g", "w_router_e",
        "b_router_e", "w_exp_gate", "w_exp_up", "w_exp_down", "ln2_g", "ln2_b"]
_OUTS = [(1, SEQ, DM), (NB, 1, DM), (1, 1, SEQ, HA, HD), (1, 1, SEQ, HA, HD), (1, NB, 1, HA, HD),
         (1, NB, 1, HA, HD), (1, 1, 128, 2, HB, HD), (1, NB, 128, 2, HB, HD), (1, 1, SEQ, 2, HB, HD),
         (1, NB, 512, 2, HB, HD), (1, 1, SEQ, 2, HB, HD), (1, NB, 2048, 2, HB, HD)]


def _bucket(dist):
    import numpy as np
    n = np.maximum(dist, 0)
    nf = np.maximum(n, 1).astype(np.float32)
    large = 16 + (np.log(nf / np.float32(16)) / np.float32(np.log(8.0)) * np.float32(16)).astype(np.int32)
    return np.where(n < 16, n, np.minimum(large, BUCKETS - 1))


def _constants():
    import numpy as np
    c = np.zeros((P, C_END), np.float32)
    c[:, C_ID:C_ID + P] = np.eye(P)
    c[:, C_TRI:C_TRI + P] = np.triu(np.ones((P, P)), 1)
    c[:, C_ONE:C_ONE + P] = 1
    c[:, C_IOTA:C_IOTA + SLOT] = np.arange(SLOT)
    c[:, C_IE:C_IE + NE] = np.arange(NE) * SLOT
    r = np.arange(96)
    c[r, C_E96 + r // HS] = 1
    c[r, C_H96 + r % HS] = 1
    for h in range(HA):
        c[h, C_BD + h * HD:C_BD + (h + 1) * HD] = 1
    i, j = np.meshgrid(np.arange(8), np.arange(8), indexing="ij")
    c[:, C_TIE:C_TIE + 64] = (j < i).reshape(-1)
    c[0:64, C_HIND] = 1
    c[64:, C_HIND + 1] = 1
    c[:, C_TOK:C_TOK + 3] = 1 + np.arange(3)[None, :] * P + np.arange(P)[:, None]

    o = np.zeros((BUCKETS + 1, O_END), np.float32)
    dist = np.arange(VLEN) - (P - 1)
    for n in range(4):
        ok = dist >= 0
        if n:
            d = DIL[n - 1]
            ok = ok & (dist % d == 0) & (dist <= P * d)
        b = np.where(ok, _bucket(dist), BUCKETS)
        o[b, O_TOE + n * VLEN + np.arange(VLEN)] = 1
    pos = np.arange(PAST)
    o[_bucket(PAST - pos), O_SMP + pos] = 1
    for g, d in enumerate(DIL):
        o[_bucket((P - np.arange(P)) * d), O_SMP + PAST + g * P + np.arange(P)] = 1
    o[0, O_ZERO:O_ZERO + NB] = 1
    return c, o, np.full((1, HALL), NEG, np.float32)


def kernel(**inputs):
    import numpy as _np
    import concourse.bacc as _bacc
    from concourse import mybir as _mybir
    from concourse.bass_utils import run_bass_kernel_spmd as _run

    nc = _bacc.Bacc("TRN2", target_bir_lowering=False, num_devices=1)
    arrays, args = {}, []
    given = {n: _np.ascontiguousarray(inputs[n]) for n in _INS}
    given.update(zip(("consts", "onehots", "negrow"), _constants()))
    for name, a in given.items():
        arrays[f"in_{name}_dram"] = a
        args.append(nc.dram_tensor(f"in_{name}_dram", a.shape, _mybir.dt.from_np(a.dtype), kind="ExternalInput").ap())
    for i, shape in enumerate(_OUTS):
        args.append(nc.dram_tensor(f"out_{i}_dram", shape, F32, kind="ExternalOutput").ap())
    trunk(nc, *args)
    r = _run(nc, [arrays], core_ids=[0])
    return tuple(r.results[0][f"out_{i}_dram"] for i in range(len(_OUTS)))
```

```python
from contextlib import ExitStack

import concourse.bass as bass
from concourse import mybir

F32 = mybir.dt.float32
I32 = mybir.dt.int32
U32 = mybir.dt.uint32
ALU = mybir.AluOpType
ACT = mybir.ActivationFunctionType
AX = mybir.AxisListType

P = 128
DM = 1024
KC = DM // P
SEQ = 256
NB = 8
NT = SEQ + NB
TT = [(0, P), (P, P), (SEQ, NB)]
HD = 64
HA = 8
HB = 4
DIL = (1, 4, 16)
NG = len(DIL)
HS = HA + HB
HALL = HA + NG * HB
AW = HA * HD
BW = NG * HB * HD
PAST = 2048
PAGE = 128
NPG = PAST // PAGE
HPG = NPG // 2
NBLK = 8
TOPK = 3
QSCALE = HD ** -0.5
BUCKETS = 32
VLEN = 384
NE = 32
EG = 8
NGRP = 4
FF = 512
FC = FF // P
SLOT = 64
MAXR = -(-NT // SLOT)
EPS = 1e-5
ALPHA = 2 ** 0.25
NEG = -1e30

QA, KA, VA, QB, KB, VB, GA, GB = 0, 4, 8, 12, 18, 24, 30, 38
C_ID, C_TRI, C_ONE, C_IOTA, C_IE, C_E96, C_H96, C_BD, C_TIE, C_HIND, C_TOK, C_HM1 = (
    0, 128, 256, 384, 448, 480, 488, 500, 1012, 1076, 1078, 1081)
C_END = 1082
NX = MAXR * NE + 4
UNR = 4
O_TOE, O_SMP, O_ZERO = 0, 4 * VLEN, 4 * VLEN + (NPG + NG) * P
O_END = O_ZERO + 8


def trunk(nc, x_prompt, x_sample, k_pages, v_pages, page_table, st1, st4, st16, c_prompt, c_sample,
          rel_bias, w_ada, b_ada, w_in, w_proj_a, w_proj_b, w_out, ln1_g, ln1_b, w_rg, b_rg, w_re,
          b_re, w_eg, w_eu, w_ed, ln2_g, ln2_b, consts, onehots, negrow,
          y_prompt, y_sample, k_prompt, v_prompt, k_sample, v_sample,
          d1p, d1s, d4p, d4s, d16p, d16s):
    ctx = ExitStack()
    with ctx:
        def sb(name, shape, dt=F32):
            return ctx.enter_context(nc.sbuf_tensor(name, shape, dt))

        def sem(name):
            return ctx.enter_context(nc.semaphore(name))

        cst = sb("cst", [P, C_END])
        ident, tri, ones = (cst[:, c:c + P] for c in (C_ID, C_TRI, C_ONE))
        iota = cst[:, C_IOTA:C_IOTA + SLOT]
        e96 = cst[0:96, C_E96:C_E96 + NB]
        h96 = cst[0:96, C_H96:C_H96 + HS]
        blkdiag = cst[:, C_BD:C_BD + AW]
        tie = cst[:, C_TIE:C_TIE + 64]
        hind = cst[:, C_HIND:C_HIND + 2]

        ring = sb("ring", [P, 6, 4096])
        x = sb("x", [P, 3, DM])
        mod = sb("mod", [P, 48, NB + 1])
        bT = sb("bT", [P, 48])
        gates = sb("gates", [P, 16 * NT])
        zT = sb("zT", [P, 20 * NT])
        v = sb("v", [P, 3, AW + BW])
        hT = sb("hT", [P, KC * NT])
        qbc = sb("qbc", [P, 4 * AW])
        S = sb("S", [P, NB * NPG * HA])
        Sd = sb("Sd", [P, NB * NG * HB])
        work = sb("work", [P, 4 * NG * SEQ])
        cT = sb("cT", [P, KC * (NB + 1) + 24])
        hs = sb("hs", [P, KC * NB])
        prod = sb("prod", [P, 10 * NB])
        own = sb("own", [NB, 64])
        m12 = sb("m12", [P, NB * HS])
        ownD = sb("ownD", [NB, NB * HS])
        st96 = sb("st96", [P, 128])
        powD = sb("powD", [NB, NB * HA + NB * NG * HB])
        rinv = sb("rinv", [P, 2 * NB])
        rel = sb("rel", [BUCKETS + 1, HALL])
        sbias = sb("sbias", [P, NPG * HA + NG * HB])
        pt = sb("pt", [1, NB * NPG], I32)
        stat = sb("stat", [P, 24])
        nst = sb("nst", [P, 3, 2])
        sdev = sb("sdev", [P, 3])
        rounds_i = sb("rounds_i", [1, 1], I32)
        rowf = sb("rowf", [P, 2, 4])
        ridx = sb("ridx", [P, UNR], U32)
        wts = sb("wts", [P, 3, 2])

        slot_wpb = 1
        hot = gates[0:BUCKETS + 1, 0:O_END]
        crow, brow_t = work[0:NB + 1, 0:DM], work[0:48, DM:DM + P]
        toev = work[0:HA, 1280:1280 + 4 * VLEN].rearrange("p (n w) -> p n w", n=4)
        modr = [work[:, 2816 + i * P:2944 + i * P] for i in range(2)]
        kst = [work[:, i * 1280:(i + 1) * 1280] for i in range(2)]
        hT3 = hT[:, :].rearrange("p (k n) -> p k n", k=KC)
        zT3 = zT[:, :].rearrange("p (c n) -> p c n", n=NT)
        oT3 = qbc[:, 0:6 * NT].rearrange("p (c n) -> p c n", n=NT)
        gates3 = gates[:, :].rearrange("p (c n) -> p c n", n=NT)
        toe_a = hT[:, 0:HA * SEQ].rearrange("p (h k) -> p h k", k=SEQ)
        toe_b = x[:, :, :].rearrange("p a b -> p (a b)").rearrange("p (h k) -> p h k", k=SEQ)
        mixT = zT3[:, 0:KC, :]
        lng, lnb, g2p = (zT[:, 8 * NT + i * DM:8 * NT + (i + 1) * DM] for i in range(3))
        g2s = qbc[0:NB, 0:DM]
        vsc = ring[:, slot_wpb, 2048:4096]
        vm = [vsc[:, i * 512:(i + 1) * 512] for i in range(2)]
        pst = [vsc[:, 1024 + i * P:1024 + (i + 1) * P] for i in range(2)]
        pst1 = [vsc[0:NB, 1280 + i * HA:1280 + (i + 1) * HA] for i in range(2)]
        odm = [vsc[0:HB, 1296 + i * 256:1296 + (i + 1) * 256] for i in range(2)]
        pk = [work[:, i * 768:(i + 1) * 768] for i in range(2)]
        pT = [work[:, 1536 + i * 768:1536 + (i + 1) * 768] for i in range(2)]
        S4 = S[:, :].rearrange("p (b k h) -> p b k h", b=NB, k=NPG)
        Sd4 = Sd[:, :].rearrange("p (b g h) -> p b g h", b=NB, g=NG)
        h2 = v[:, :, 0:DM]
        xg = gates[:, 0:512]
        xT = gates[:, 512:1024].rearrange("p (k s) -> p k s", s=SLOT)
        sg, act_g, aT = (gates[:, 1024 + i * 256:1280 + i * 256] for i in range(3))
        G = [gates[:, 1792 + i * 192:1984 + i * 192].rearrange("p (t n) -> p t n", t=3) for i in range(2)]
        yrow = [work[:, i * 512:(i + 1) * 512] for i in range(UNR)]
        posx, rowx = (S[:, i * 3 * NX:(i + 1) * 3 * NX].rearrange("p (t e) -> p t e", t=3) for i in range(2))

        bank = [ctx.enter_context(nc.psum_tensor(f"bank{i}", [P, 512], F32)) for i in range(8)]
        full = [sem(f"bank{i}_full") for i in range(8)]
        free = [sem(f"bank{i}_free") for i in range(8)]

        toe_d = nc.dram_tensor("toe_scratch", [HALL * VLEN], F32)
        ys_d = nc.dram_tensor("expert_rows", [4 * NT, DM // 2], F32)

        s_cst, s_hot, s_c, s_bt, s_x, s_pt, s_x2, s_wr, s_rb, s_ln1, = (sem(n) for n in "s_cst s_hot s_c s_bt s_x s_pt s_x2 s_wr s_rb s_ln1".split())
        s_silu, s_cT, s_bT, s_modr, s_mod, = (sem(n) for n in "s_silu s_cT s_bT s_modr s_mod".split())
        s_norm, s_hTp, s_hs, s_hTs, = (sem(n) for n in "s_norm s_hTp s_hs s_hTs".split())
        s_var, s_sd, = (sem(n) for n in "s_var s_sd".split())
        s_z, s_vrow, s_qbc, s_kst, = (sem(n) for n in "s_z s_vrow s_qbc s_kst".split())
        s_toev, s_toes, s_toeb, s_toea, = (sem(n) for n in "s_toev s_toes s_toeb s_toea".split())
        s_kmul, s_kred, s_kdmul, s_kdred, s_prod, s_own, s_sbias, = (sem(n) for n in "s_kmul s_kred s_kdmul s_kdred s_prod s_own s_sbias".split())
        s_pen, s_m12, s_ownx, s_negm, s_sub, s_exp, s_sum, s_rec, s_rs, = (sem(n) for n in "s_pen s_m12 s_ownx s_negm s_sub s_exp s_sum s_rec s_rs".split())
        s_pst, s_vm, s_oa, s_odt, s_vhi, = (sem(n) for n in "s_pst s_vm s_oa s_odt s_vhi".split())
        s_lg, s_pexp, s_pn, s_pT, s_po, = (sem(n) for n in "s_lg s_pexp s_pn s_pT s_po".split())
        s_u, s_mix, s_x1, s_n2, s_g2, = (sem(n) for n in "s_u s_mix s_x1 s_n2 s_g2".split())
        s_h2T, s_h2, s_rlg, s_rexp, s_mask, s_round, = (sem(n) for n in "s_h2T s_h2 s_rlg s_rexp s_mask s_round".split())
        s_G, s_xg, s_xgs, s_xgT, s_xT, = (sem(n) for n in "s_G s_xg s_xgs s_xgT s_xT".split())
        s_gu, s_sg, s_act, s_aTp, s_aT, s_yt, s_yrow, = (sem(n) for n in "s_gu s_sg s_act s_aTp s_aT s_yt s_yrow".split())
        s_big, s_idx, s_scat, s_rows, = (sem(n) for n in "s_big s_idx s_scat s_rows".split())
        s_y, s_out, s_st, s_vout, = (sem(n) for n in "s_y s_out s_st s_vout".split())
        s_dve, s_pool, = (sem(n) for n in "s_dve s_pool".split())
        s_vread = [sem("s_vread0"), sem("s_vread1")]
        s_gat = [sem(f"s_gat{t}") for t in range(3)]
        s_kout = [sem("s_kout0"), sem("s_kout1")]
        s_yst = [sem(f"s_yst{i}") for i in range(UNR)]
        w_full = [sem(f"w_full{i}") for i in range(6)]
        ew_full = [sem(f"ew_full{i}") for i in range(6)]

        turn, uses = {}, [0] * 8

        def chain(eng, s):
            n = [0]

            def link(ins):
                n[0] += 1
                ins.then_inc(s, 1)
                eng.wait_ge(s, n[0])
            return link

        ring_use, slot_n, slot_v = {}, [0] * 6, [0] * 6

        def ring_take(name, slot, dmas=1):
            slot_v[slot] += 16 * dmas
            ring_use[name] = (slot, slot_n[slot], slot_v[slot])
            slot_n[slot] += 1

        weights = [("ada", t) for t in range(4)] + [("win", t) for t in range(12)] \
            + [("ada", t) for t in range(4, 12)] + [("wpa", 0), ("wpb", 0), ("wo", 0), ("wo", 1)]
        for n, name in enumerate(weights):
            ring_take(name, n % 4)
        for b in range(NB):
            ring_take(("k", b, 0), 4, HPG)
            ring_take(("k", b, 1), 5, HPG)
        for g in range(NG):
            ring_take(("kd", g), 4 + g % 2)
        v_val0 = slot_v[4]
        for b in range(NB):
            ring_take(("v", b, 0), 4, HPG)
        ring_take(("vd", 0), 4, 2)
        ring_take(("vd", 2), 5)

        assert ring_use[("wpb", 0)][0] == slot_wpb

        def slot_of(name):
            return ring_use[name][0]

        def landed(eng, name):
            slot, _, val = ring_use[name]
            eng.wait_ge(w_full[slot], val)
            return ring[:, slot, :]

        last_use = {}

        def filled(eng, key):
            b, n = turn[key]
            eng.wait_ge(full[b], n + 1)
            return bank[b]

        states, st_out, st_p = (st1, st4, st16), (d1s, d4s, d16s), (d1p, d4p, d16p)
        V_TILES = {2: (0, 512), 6: (AW, 512), 7: (AW + 512, 256)}
        Q_AFTER = {0: (0, 1, 2, 3), 3: (4,), 5: (5,), 6: (6,), 7: (7,)}
        ZROW = {c: n for n, c in enumerate([*range(QA, VA), *range(QB, VB)])}
        KT = ((ZROW[KA], 4, 0), (ZROW[KB], 3, AW), (ZROW[KB + 3], 3, AW + 384))
        units = [("a", h, qt) for h in range(HA) for qt in range(2)] + \
                [("b", h, qt) for h in range(HB) for qt in range(2)]

        def heads(u):
            kind, h, _ = u
            if kind == "a":
                return [(ZROW[QA] + h // 2, ZROW[KA] + h // 2, h % 2, h * HD)]
            return [(ZROW[QB] + (g * HB + h) // 2, ZROW[KB] + (g * HB + h) // 2, h % 2, AW + (g * HB + h) * HD)
                    for g in range(NG)]

        def load_pages(eng, cache, b, hh, landed_):
            for k in range(HPG):
                page = eng.value_load(pt[0:1, bass.ds(b * NPG + (hh * HPG + k), 1)], min_val=0, max_val=cache.shape[1] - 1)
                src = cache[0, bass.ds(page, 1)].rearrange("o t h d -> (o t) (h d)")
                eng.dma_start(ring[:, 4 + hh, k * AW:(k + 1) * AW], src).then_inc(landed_, 16)

        block = ctx.enter_context(nc.Block())

        @block.tensor
        def _(pe):
            mm, tr = nc.tensor.matmul, nc.tensor.transpose

            def take(key, b):
                turn[key] = (b, uses[b])
                if uses[b]:
                    pe.wait_ge(free[b], uses[b])
                uses[b] += 1
                return bank[b]

            def done(key, ins):
                ins.then_inc(full[turn[key][0]], 1)

            pe.wait_ge(s_cst, 16)
            pe.wait_ge(s_silu, 1)
            bk = take("cT", 2)
            for k in range(KC):
                i = tr(bk[:, k * 9:(k + 1) * 9], crow[:, k * P:(k + 1) * P], ident[0:9, 0:9])
            done("cT", i)
            pe.wait_ge(s_bt, 16)
            bk = take("bT", 3)
            done("bT", tr(bk[:, 0:48], brow_t, ident[0:48, 0:48]))

            def ada(tiles):
                for t in [*tiles, None]:
                    if t is not None:
                        w = landed(pe, ("ada", t)).rearrange("p (k n) -> p k n", k=KC)
                        bk = take(("adr", t), t % 2)
                        for k in range(KC):
                            for j in range(4):
                                i = mm(bk[32 * j:32 * j + 32, 0:P], cT[:, k * 9:k * 9 + 32], w[:, k, j * P:(j + 1) * P],
                                       start=(k == 0), stop=(k == KC - 1))
                        done(("adr", t), i)
                        last_use[("ada", t)] = ("adr", t)
                    before = tiles[-1] if t is None else t - 1
                    if before in tiles:
                        pe.wait_ge(s_modr, before + 1)
                        bk = take(("ada", before), 6 + before % 2)
                        done(("ada", before), tr(bk[:, 0:P], modr[before % 2], ident))

            pe.wait_ge(s_cT, 2)
            ada(range(4))

            for t, (t0, tn) in enumerate(TT):
                pe.wait_ge(s_norm, t + 1)
                for h in range(2):
                    bk = take(("xT", t, h), 2 + h)
                    for j in range(4):
                        k = 4 * h + j
                        i = tr(bk[:, j * P:j * P + tn], x[0:tn, t, k * P:(k + 1) * P], ident[0:tn, 0:tn])
                    done(("xT", t, h), i)

            pe.wait_ge(s_hot, 48)
            bk = take("sbias", 4)
            for p in range(NPG):
                mm(bk[:, p * HA:(p + 1) * HA], hot[:, O_SMP + p * P:O_SMP + (p + 1) * P], rel[:, 0:HA],
                   start=True, stop=True)
            for g in range(NG):
                c = O_SMP + (NPG + g) * P
                i = mm(bk[:, NPG * HA + g * HB:NPG * HA + (g + 1) * HB], hot[:, c:c + P],
                       rel[:, HA + g * HB:HA + (g + 1) * HB], start=True, stop=True)
            done("sbias", i)
            for n in range(4):
                h0, hn = (0, HA) if n == 0 else (HA + (n - 1) * HB, HB)
                bk = take(("toev", n), 5)
                done(("toev", n), mm(bk[0:hn, 0:VLEN], rel[:, h0:h0 + hn],
                                     hot[:, O_TOE + n * VLEN:O_TOE + (n + 1) * VLEN], start=True, stop=True))

            pe.wait_ge(s_hTp, 2)
            pe.wait_ge(s_hTs, 1)
            acc = [0]

            def win_T(w, c, j):
                bk = take(("z", c), acc[0] % 2)
                acc[0] += 1
                for k in range(KC):
                    i = mm(bk[:, 0:NT], w[:, k, j * P:(j + 1) * P], hT3[:, k, :], start=(k == 0), stop=(k == KC - 1))
                done(("z", c), i)
                return i

            def win_v(w, c0, n):
                for t, (t0, tn) in enumerate(TT):
                    bk = take(("v", c0, t), acc[0] % 2)
                    acc[0] += 1
                    for k in range(KC):
                        i = mm(bk[0:tn, 0:n], hT3[:, k, t0:t0 + tn], w[:, k, 0:n], start=(k == 0), stop=(k == KC - 1))
                    done(("v", c0, t), i)
                return i

            def spread(row, b):
                return zT3[:, row, SEQ + b:SEQ + b + 1].to_broadcast([P, P])

            for t in range(12):
                name = ("win", t)
                width = 512 if t < 11 else 256
                w = landed(pe, name)[:, 0:KC * width].rearrange("p (k n) -> p k n", k=KC)
                if t in V_TILES:
                    i = win_v(w, *V_TILES[t])
                for j in range(V_TILES[t][1] // P if t in V_TILES else 0, width // P):
                    i = win_T(w, 4 * t + j, j)
                last_use[name] = ("z", 4 * t + 3) if t not in (2, 6) and t < 11 else \
                    ("z", 45) if t == 11 else ("v", V_TILES[t][0], 2)
                for b in Q_AFTER.get(t, ()):
                    pe.wait_ge(s_z, 4)
                    bk = take(("qbc", b), 2 + b % 2)
                    for j in range(4):
                        i = mm(bk[:, j * P:(j + 1) * P], spread(ZROW[QA] + j, b), ident, start=True, stop=True)
                    done(("qbc", b), i)
                if t == 5:
                    pe.wait_ge(s_z, 20)
                    for tt, (t0, tn) in enumerate(TT):
                        for n, (r0, rn, _) in enumerate(KT):
                            bk = take(("kt", tt, n), 2 + (tt * 3 + n) % 2)
                            for j in range(rn):
                                i = tr(bk[0:tn, j * P:(j + 1) * P], zT3[:, r0 + j, t0:t0 + tn], ident)
                            done(("kt", tt, n), i)
                    pe.wait_ge(s_prod, 1)
                    bk = take("own", 5)
                    for c in range(10):
                        mm(bk[0:NB, 2 * c:2 * c + 2], prod[:, c * NB:(c + 1) * NB], hind, start=True, stop=True)
                    done("own", mm(bk[0:NB, HALL:2 * HALL], hot[:, O_ZERO:O_ZERO + NB], rel[:, :], start=True, stop=True))
            for g in range(NG):
                for b in range(NB):
                    bk = take(("qbd", g, b), 2 + b % 2)
                    for j in range(2):
                        i = mm(bk[:, j * P:(j + 1) * P], spread(ZROW[QB] + 2 * g + j, b), ident, start=True, stop=True)
                    done(("qbd", g, b), i)

            pe.wait_ge(s_kred, 2 * NB)
            for h in range(2):
                bk = take(("bs", h), 4 + h)
                done(("bs", h), mm(bk[0:NB, :], ones[:, 0:NB], S[:, h * 512:(h + 1) * 512], start=True, stop=True))
            ada(range(4, 6))
            pe.wait_ge(s_pen, 1)
            bk = take("pen", 4)
            done("pen", mm(bk[:, :], ones[0:NB, :], work[0:NB, 2048:2560], start=True, stop=True))
            ada(range(6, 8))
            pe.wait_ge(s_m12, 1)
            bk = take("mxT", 5)
            done("mxT", tr(bk[0:96, 0:P], m12[:, :], ident))
            ada(range(8, 10))
            pe.wait_ge(s_ownx, 1)
            bk = take("ownx", 4)
            done("ownx", mm(bk[0:96, 0:1], ownD[:, :], ones[0:NB, 0:1], start=True, stop=True))
            ada(range(10, 12))
            pe.wait_ge(s_negm, 1)
            bk = take("negm", 5)
            mm(bk[:, 0:96], ones[0:96, :], st96[0:96, 0:96], start=True, stop=True)
            done("negm", mm(bk[0:NB, 96:96 + HS], e96, st96[0:96, 96:96 + HS], start=True, stop=True))
            pe.wait_ge(s_sum, 1)
            bk = take("sum", 4)
            mm(bk[0:96, 0:1], m12[:, :], ones[:, 0:1], start=True, stop=False)
            done("sum", mm(bk[0:96, 0:1], ownD[:, :], ones[0:NB, 0:1], start=False, stop=True))
            pe.wait_ge(s_rec, 1)
            bk = take("rs", 5)
            mm(bk[:, 0:NB], work[0:96, 2560:2688], st96[0:96, 0:NB], start=True, stop=True)
            done("rs", mm(bk[0:HB, NB:2 * NB], h96[:, HA:HS], st96[0:96, 0:NB], start=True, stop=True))

            def sample_values(b, hh):
                if hh == 0:
                    pe.wait_ge(s_pst, b + 1)
                    take(("ov", b), 6)
                bk = bank[6]
                vt = ring[:, 4 + hh, :].rearrange("p (k n) -> p k n", k=HPG)
                pe.wait_ge((w_full[4], s_vhi)[hh], (v_val0, 0)[hh] + (b + 1) * 16 * HPG)
                for k in range(HPG):
                    q, j = (hh * HPG + k) // 4, k % 4
                    i = mm(bk[32 * j:32 * j + 32, :], pst[b % 2][:, 32 * q:32 * q + 32], vt[:, k, :],
                           start=(q == 0), stop=(q == 3 and j > 0))
                i.then_inc(s_vread[hh], 1)
                if hh == 1:
                    done(("ov", b), mm(bk[0:HA, :], pst1[b % 2], v[0:NB, 2, 0:AW], start=False, stop=True))

            def sample_columns(b):
                pe.wait_ge(s_vm, b + 1)
                bk = take(("vt", b), 7)
                for c in range(4):
                    i = mm(bk[:, c:c + 1], vm[b % 2][:, c * P:(c + 1) * P], rinv[:, b:b + 1], start=True, stop=True)
                done(("vt", b), i)

            def scores(n):
                u = units[n]
                nk = P * (u[2] + 1)
                for gi, (qr, kr, par, _) in enumerate(heads(u)):
                    bk = take(("sc", n, gi), 4 + (n + gi) % 2)
                    done(("sc", n, gi), mm(bk[:, 0:nk], zT3[par * HD:(par + 1) * HD, qr, u[2] * P:(u[2] + 1) * P],
                                           zT3[par * HD:(par + 1) * HD, kr, 0:nk], start=True, stop=True))

            def turn_weights(n):
                u = units[n]
                nk = P * (u[2] + 1)
                pe.wait_ge(s_pn, n + 1)
                for gi in range(len(heads(u))):
                    bk = take(("pt", n, gi), 2 + (n + gi) % 2)
                    for kt in range(u[2] + 1):
                        c = gi * nk + kt * P
                        i = tr(bk[:, kt * P:(kt + 1) * P], pk[n % 2][:, c:c + P], ident)
                    done(("pt", n, gi), i)

            def values(n):
                u = units[n]
                hh = heads(u)
                pe.wait_ge(s_pT, n + 1)
                bk = take(("po", n), n % 2)
                par = u[1] % 2
                for gi, (_, _, _, vc) in enumerate(hh):
                    for kt in range(u[2] + 1):
                        i = mm(bk[par * HD:(par + 1) * HD, 0:P], v[:, kt, vc:vc + HD],
                               pT[n % 2][:, gi * SEQ + kt * P:gi * SEQ + (kt + 1) * P],
                               start=(gi == 0 and kt == 0), stop=(gi == len(hh) - 1 and kt == u[2]))
                done(("po", n), i)

            pe.wait_ge(s_rs, 1)
            for n in range(len(units) + 2):
                if n < len(units):
                    scores(n)
                if 1 <= n <= len(units):
                    turn_weights(n - 1)
                if n >= 2:
                    values(n - 2)
                if n % 3 and n < len(units):
                    sample_values(n // 3, n % 3 - 1)
                if n % 3 == 1 and n >= 4:
                    sample_columns(n // 3 - 1)

            pe.wait_ge(s_oa, NB)
            vd0 = landed(pe, ("vd", 0)).rearrange("p (g b n) -> p g b n", g=2, b=NB)
            vd2 = landed(pe, ("vd", 2))[:, 0:2048].rearrange("p (b n) -> p b n", b=NB)
            odT = take("odT", 4)
            for b in range(NB + 1):
                if b < NB:
                    bk = take(("od", b), 6 + b % 2)
                    for g in range(NG):
                        r = vd0[:, g, b, :] if g < 2 else vd2[:, b, :]
                        mm(bk[0:HB, 0:256], Sd4[:, b, g, :], r, start=(g == 0), stop=False)
                    for g in range(NG):
                        c = NB * HA + (b * NG + g) * HB
                        i = mm(bk[0:HB, 0:256], powD[:, c:c + HB], v[0:NB, 2, AW + g * 256:AW + (g + 1) * 256],
                               start=False, stop=(g == NG - 1))
                    done(("od", b), i)
                if b >= 1:
                    a = b - 1
                    pe.wait_ge(s_vm, NB + a + 1)
                    for c in range(2):
                        i = mm(odT[:, c * NB + a:c * NB + a + 1], odm[a % 2][:, c * P:(c + 1) * P],
                               rinv[0:HB, NB + a:NB + a + 1], start=True, stop=True)
                    if a < NB - 1:
                        i.then_inc(s_odt, 1)
            done("odT", i)
            last_use[("vd", 0)] = last_use[("vd", 2)] = ("od", NB - 1)

            pe.wait_ge(s_po, len(units))
            pe.wait_ge(s_oa, NB + 1)
            wa = landed(pe, ("wpa", 0)).rearrange("p (k n) -> p k n", k=4)
            wb = landed(pe, ("wpb", 0))[:, 0:2048].rearrange("p (k n) -> p k n", k=2)
            for j in range(KC):
                bk = take(("ya", j), j % 2)
                for k in range(4):
                    i = mm(bk[:, 0:NT], wa[:, k, j * P:(j + 1) * P], oT3[:, k, :], start=(k == 0), stop=(k == 3))
                done(("ya", j), i)
                bk = take(("yb", j), 2 + j % 2)
                for k in range(2):
                    i = mm(bk[:, 0:NT], wb[:, k, j * P:(j + 1) * P], oT3[:, 4 + k, :], start=(k == 0), stop=(k == 1))
                done(("yb", j), i)
            last_use[("wpa", 0)] = last_use[("wpb", 0)] = ("yb", KC - 1)
            pe.wait_ge(s_u, KC)
            for j in range(KC):
                half = ("wo", j // 4)
                w = landed(pe, half).rearrange("p (k n) -> p k n", k=KC)
                bk = take(("mix", j), j % 2)
                for k in range(KC):
                    i = mm(bk[:, 0:NT], w[:, k, (j % 4) * P:(j % 4 + 1) * P], hT3[:, k, :],
                           start=(k == 0), stop=(k == KC - 1))
                done(("mix", j), i)
                last_use[half] = ("mix", j)
            pe.wait_ge(s_mix, KC)
            for t, (t0, tn) in enumerate(TT):
                for h in range(2):
                    bk = take(("mt", t, h), 2 + h)
                    for j in range(4):
                        i = tr(bk[0:tn, j * P:(j + 1) * P], mixT[:, 4 * h + j, t0:t0 + tn], ident)
                    done(("mt", t, h), i)

            for h in range(2):
                bk = take(("g2", h), 6)
                for j in range(4):
                    i = mm(bk[:, j * P:(j + 1) * P], mod[:, 40 + 4 * h + j, NB:NB + 1].to_broadcast([P, P]), ident,
                           start=True, stop=True)
                done(("g2", h), i)
                bk = take(("g2s", h), 7)
                for j in range(4):
                    i = tr(bk[0:NB, j * P:(j + 1) * P], mod[:, 40 + 4 * h + j, 0:NB], ident)
                done(("g2s", h), i)
            for t, (t0, tn) in enumerate(TT):
                pe.wait_ge(s_n2, t + 1)
                for h in range(2):
                    bk = take(("nT", t, h), 4 + h)
                    for j in range(4):
                        k = 4 * h + j
                        i = tr(bk[:, j * P:j * P + tn], h2[0:tn, t, k * P:(k + 1) * P], ident[0:tn, 0:tn])
                    done(("nT", t, h), i)
            pe.wait_ge(s_wr, 5 * 16)
            pe.wait_ge(s_h2T, 3)
            bk = take("lg", 2)
            wr = work[:, 2700:2700 + KC * 36].rearrange("p (k n) -> p k n", k=KC)
            for t, (t0, tn) in enumerate(TT):
                for k in range(KC):
                    i = mm(bk[0:tn, t * 36:(t + 1) * 36], hT3[:, k, t0:t0 + tn], wr[:, k, :],
                           start=(k == 0), stop=(k == KC - 1))
            done("lg", i)
            for t, (t0, tn) in enumerate(TT):
                for h in range(2):
                    bk = take(("h2", t, h), h)
                    for j in range(4):
                        i = tr(bk[0:tn, j * P:(j + 1) * P], hT3[:, 4 * h + j, t0:t0 + tn], ident)
                    done(("h2", t, h), i)
            pe.wait_ge(s_mask, 1)
            M = work[:, 0:3 * NE].rearrange("p (t e) -> p t e", t=3)
            bk = take("pos", 3)
            mm(bk[:, 0:32], tri, M[:, 0, :], start=True, stop=True)
            mm(bk[:, 32:64], ones, M[:, 0, :], start=True, stop=False)
            mm(bk[:, 32:64], tri, M[:, 1, :], start=False, stop=True)
            mm(bk[0:NB, 64:96], ones[:, 0:NB], M[:, 0, :], start=True, stop=False)
            mm(bk[0:NB, 64:96], ones[:, 0:NB], M[:, 1, :], start=False, stop=False)
            mm(bk[0:NB, 64:96], tri[0:NB, 0:NB], M[0:NB, 2, :], start=False, stop=True)
            mm(bk[0:1, 96:128], ones[:, 0:1], M[:, 0, :], start=True, stop=False)
            mm(bk[0:1, 96:128], ones[:, 0:1], M[:, 1, :], start=False, stop=False)
            done("pos", mm(bk[0:1, 96:128], ones[0:NB, 0:1], M[0:NB, 2, :], start=False, stop=True))

            for b in range(8):
                pe.wait_ge(free[b], uses[b])

            def side(b, half):
                return bank[b][half * SLOT:(half + 1) * SLOT, :]

            def gather(s, nth):
                pe.wait_ge(s_G, nth)
                pe.wait_ge(s_idx, nth)
                for half in range(2):
                    for t, (t0, tn) in enumerate(TT):
                        mm(side(5, half)[:, 0:1], G[s][0:tn, t, :], rowf[0:tn, s, t:t + 1], start=(t == 0), stop=(t == 2))
                for t, (t0, tn) in enumerate(TT):
                    for half in range(2):
                        i = mm(side(0, half), G[s][0:tn, t, :], h2[0:tn, t, half * 512:(half + 1) * 512],
                               start=(t == 0), stop=(t == 2))
                i.then_inc(s_xg, 1)

            def turn_tokens(nth):
                pe.wait_ge(s_xgs, nth)
                for j in range(4):
                    i = tr(bank[1][:, j * P:(j + 1) * P], xg[:, j * P:(j + 1) * P], ident)
                i.then_inc(s_xgT, 1)

            def gate_up(s, nth, load):
                pe.wait_ge(s_xT, nth)
                pe.wait_ge(ew_full[3 * s], load)
                pe.wait_ge(ew_full[3 * s + 1], load)
                w = ring[:, 3 * s:3 * s + 2, :].rearrange("p m (k n) -> p m k n", k=KC)
                for k in range(KC):
                    for half in range(2):
                        i = mm(side(2, half).rearrange("p (m n) -> p m n", m=2), xT[:, 2 * (k % 4) + k // 4, :],
                               w[:, :, k, half * 256:(half + 1) * 256], start=(k == 0), stop=(k == KC - 1))
                i.then_inc(s_gu, 1)

            def turn_acts(nth):
                pe.wait_ge(s_act, nth)
                for f in range(2):
                    i = tr(bank[3][:, f * P:(f + 1) * P], act_g[:, f * P:(f + 1) * P], ident)
                i.then_inc(s_aTp, 1)

            def down(s, nth, load):
                w = ring[:, 3 * s + 2, :].rearrange("p (f n) -> p f n", f=FC)
                pe.wait_ge(ew_full[3 * s + 2], load)
                pe.wait_ge(s_yrow, nth)
                pe.wait_ge(s_aT, nth)
                for f in range(FC):
                    a = (f % 2) * P + (f // 2) * SLOT
                    for half in range(2):
                        i = mm(side(4, half), aT[:, a:a + SLOT], w[:, f, half * 512:(half + 1) * 512],
                               start=(f == 0), stop=(f == FC - 1))
                i.then_inc(s_yt, 1)

            pe.wait_ge(s_round, 2)
            n_r = pe.value_load(rounds_i[0:1, 0:1], min_val=1, max_val=MAXR)
            gather(0, 1)
            turn_tokens(1)
            gather(1, 2)
            with pe.Fori(0, n_r * (NE // UNR)) as i4:
                for u in range(UNR):
                    n, load = UNR * i4 + u + 1, i4 * (16 * UNR // 2) + (16 + 16 * (u // 2))
                    gate_up(u % 2, n, load)
                    turn_tokens(n + 1)
                    turn_acts(n)
                    gather(u % 2, n + 2)
                    down(u % 2, n, load)

        @block.scalar
        def _(act):
            A = nc.scalar.activation

            def copy(out, in_):
                return A(out, in_, ACT.Copy)

            def freed(key, ins, also=None):
                b, n = turn[key]
                ins.then_inc(free[b], 1)
                if also is not None:
                    act.wait_ge(free[b], n + 1)
                    act.sem_inc(also, 1)

            act.wait_ge(s_c, 32)
            A(crow, crow, ACT.Silu).then_inc(s_silu, 1)
            bk = filled(act, "cT")
            i = copy(cT[:, 0:72], bk[:, 0:72])
            freed("cT", i, s_cT)
            bk = filled(act, "bT")
            i = copy(bT[:, :], bk[:, 0:48])
            freed("bT", i, s_bt)

            def root(n):
                act.wait_ge(s_var, n)
                A(sdev[:, :], sdev[:, :], ACT.Sqrt).then_inc(s_sd, 1)

            root(1)

            def ada(tiles):
                for t in [*tiles, None]:
                    if t is not None:
                        bk = filled(act, ("adr", t))
                        freed(("adr", t), copy(modr[t % 2], bk[:, 0:P]), s_modr)
                    before = tiles[-1] if t is None else t - 1
                    if before in tiles:
                        bk = filled(act, ("ada", before))
                        if before == 0:
                            act.wait_ge(s_bT, 1)
                        for j in range(4):
                            c = 4 * before + j
                            i = A(mod[:, c, :], bk[:, 32 * j:32 * j + 9], ACT.Identity, bias=bT[:, c:c + 1])
                        freed(("ada", before), i, s_mod)

            ada(range(4))
            act.wait_ge(s_mod, 4)
            for t in range(2):
                for h in range(2):
                    bk = filled(act, ("xT", t, h))
                    for j in range(4):
                        k = 4 * h + j
                        i = A(hT3[:, k, t * P:(t + 1) * P], bk[:, j * P:(j + 1) * P], ACT.Identity,
                              bias=mod[:, k, NB:NB + 1], scale=mod[:, 8 + k, NB:NB + 1])
                    freed(("xT", t, h), i, s_hTp if h else None)
            hs3 = hs[:, :].rearrange("p (k n) -> p k n", k=KC)
            for h in range(2):
                bk = filled(act, ("xT", 2, h))
                i = copy(hs3[:, 4 * h:4 * h + 4, :], bk[:, :].rearrange("p (k n) -> p k n", k=4)[:, :, 0:NB])
                freed(("xT", 2, h), i, s_hs if h else None)
            bk = filled(act, "sbias")
            i = copy(sbias[:, :], bk[:, 0:NPG * HA + NG * HB])
            freed("sbias", i, s_sbias)
            for n in range(4):
                hn = HA if n == 0 else HB
                bk = filled(act, ("toev", n))
                i = copy(toev[0:hn, n, :], bk[0:hn, 0:VLEN])
                freed(("toev", n), i, s_toev)

            def state_copies(t):
                if t < NB:
                    jobs = [(2, t)]
                elif t == NB:
                    jobs = [(1, b) for b in range(NB)]
                else:
                    jobs = [(0, b) for b in range(NB)]
                for g, b in jobs:
                    n = (P * DIL[g] - 1) // 16
                    src = states[g][0, b].rearrange("w a h d -> (w a h d)")
                    dst = st_out[g][0, b].rearrange("w a h d -> (w a h d)")
                    m = 16 * n * 512
                    act.dma_start(dst[0:m].rearrange("(a m) -> a m", a=16),
                                  src[512:512 + m].rearrange("(a m) -> a m", a=16)).then_inc(s_st, 16)
                if t >= NB:
                    for g in ((1,) if t == NB else (0, 2)):
                        w = P * DIL[g]
                        n = (w - 1) // 16 * 16
                        act.dma_start(st_out[g][0, :, n:w - 1].rearrange("b w a h d -> b (w a h d)"),
                                      states[g][0, :, n + 1:w].rearrange("b w a h d -> b (w a h d)")).then_inc(s_st, 16)

            for t in range(12):
                width = 512 if t < 11 else 256
                j0 = 0
                if t in V_TILES:
                    c0, cn = V_TILES[t]
                    j0 = cn // P
                    for tt, (t0, tn) in enumerate(TT):
                        bk = filled(act, ("v", c0, tt))
                        i = copy(v[0:tn, tt, c0:c0 + cn], bk[0:tn, 0:cn])
                        freed(("v", c0, tt), i, s_vrow)
                for j in range(j0, width // P):
                    c = 4 * t + j
                    bk = filled(act, ("z", c))
                    if c in ZROW:
                        freed(("z", c), copy(zT3[:, ZROW[c], :], bk[:, 0:NT]), s_z)
                    else:
                        freed(("z", c), A(gates3[:, c - GA, :], bk[:, 0:NT], ACT.Sigmoid))
                for b in Q_AFTER.get(t, ()):
                    bk = filled(act, ("qbc", b))
                    if b >= 4:
                        act.wait_ge(s_kred, 2 * (b - 3))
                    i = A(qbc[:, (b % 4) * AW:(b % 4 + 1) * AW], bk[:, :], ACT.Copy, scale=QSCALE)
                    freed(("qbc", b), i, s_qbc)
                if t == 5:
                    for tt, (t0, tn) in enumerate(TT):
                        st = kst[tt % 2]
                        if tt == 0:
                            act.wait_ge(s_toes, 64)
                        if tt == 2:
                            act.wait_ge(s_kout[0], 4 * 16)
                        for n, (_, rn, c0) in enumerate(KT):
                            bk = filled(act, ("kt", tt, n))
                            i = copy(st[0:tn, c0:c0 + rn * P], bk[0:tn, 0:rn * P])
                            freed(("kt", tt, n), i, s_kst)
                        act.wait_ge(s_kst, 3 * (tt + 1))
                        ks = s_kout[tt % 2]
                        if tt < 2:
                            act.dma_start(k_prompt[0, 0, t0:t0 + tn].rearrange("s h d -> s (h d)"), st[0:tn, 0:AW]).then_inc(ks, 16)
                            for g in range(NG):
                                if g == 0 and tt == 0:
                                    continue
                                r0 = 0 if g == 0 else t0
                                act.dma_start(st_p[g][0, 0, r0:r0 + tn, 0].rearrange("s h d -> s (h d)"),
                                              st[0:tn, AW + g * 256:AW + (g + 1) * 256]).then_inc(ks, 16)
                            if tt == 0:
                                act.dma_start(v_prompt[0, 0, 0:P].rearrange("s h d -> s (h d)"), v[:, 0, 0:AW]).then_inc(ks, 16)
                        else:
                            act.dma_start(k_sample[0, :, 0].rearrange("s h d -> s (h d)"), st[0:tn, 0:AW]).then_inc(ks, 16)
                            for g in range(NG):
                                act.dma_start(st_out[g][0, :, P * DIL[g] - 1, 0].rearrange("s h d -> s (h d)"),
                                              st[0:tn, AW + g * 256:AW + (g + 1) * 256]).then_inc(ks, 16)
                    bk = filled(act, "own")
                    i = copy(own[:, 0:2 * HALL], bk[0:NB, 0:2 * HALL])
                    freed("own", i, s_own)
            act.wait_ge(s_vrow, 9)
            act.dma_start(v_prompt[0, 0, P:SEQ].rearrange("s h d -> s (h d)"), v[:, 1, 0:AW]).then_inc(s_vout, 16)
            act.dma_start(v_sample[0, :, 0].rearrange("s h d -> s (h d)"), v[0:NB, 2, 0:AW]).then_inc(s_vout, 16)
            for g in range(NG):
                c = AW + g * 256
                if g:
                    act.dma_start(st_p[g][0, 0, 0:P, 1].rearrange("s h d -> s (h d)"), v[:, 0, c:c + 256]).then_inc(s_vout, 16)
                r0 = 0 if g == 0 else P
                act.dma_start(st_p[g][0, 0, r0:r0 + P, 1].rearrange("s h d -> s (h d)"), v[:, 1, c:c + 256]).then_inc(s_vout, 16)
                act.dma_start(st_out[g][0, :, P * DIL[g] - 1, 1].rearrange("s h d -> s (h d)"), v[0:NB, 2, c:c + 256]).then_inc(s_vout, 16)
            for g in range(NG):
                for b in range(NB):
                    bk = filled(act, ("qbd", g, b))
                    if b == 0:
                        act.wait_ge(s_kred, 2 * NB) if g == 0 else act.wait_ge(s_kdred, g)
                    i = A(qbc[:, b * 256:(b + 1) * 256], bk[:, 0:256], ACT.Copy, scale=QSCALE)
                    freed(("qbd", g, b), i, s_qbc)

            for t in range(4, 12, 2):
                ada(range(t, t + 2))
            state_copies(0)
            act.wait_ge(s_sub, 1)
            A(S[:, :], S[:, :], ACT.Exp).then_inc(s_exp, 1)
            A(Sd[:, :], Sd[:, :], ACT.Exp).then_inc(s_exp, 1)
            A(own[:, 40:60], own[:, 40:60], ACT.Exp).then_inc(s_exp, 1)
            act.wait_ge(s_rs, 1)
            def stage(b):
                if b >= 2:
                    filled(act, ("ov", b - 2))
                copy(pst[b % 2], S[:, b * NPG * HA:(b + 1) * NPG * HA])
                copy(pst1[b % 2], powD[:, b * HA:(b + 1) * HA]).then_inc(s_pst, 1)

            for b in range(2):
                stage(b)

            for n in range(len(units) + 1):
                if n < len(units):
                    u = units[n]
                    w = len(heads(u)) * P * (u[2] + 1)
                    act.wait_ge(s_lg, n + 1)
                    A(pk[n % 2][:, 0:w], pk[n % 2][:, 0:w], ACT.Exp, bias=stat[:, n % 2:n % 2 + 1],
                      accum_out=stat[:, 2 + n % 2:3 + n % 2]).then_inc(s_pexp, 1)
                if n >= 1:
                    m = n - 1
                    u = units[m]
                    nk = P * (u[2] + 1)
                    if m >= 2:
                        act.wait_ge(s_po, m - 1)
                    for gi in range(len(heads(u))):
                        bk = filled(act, ("pt", m, gi))
                        i = copy(pT[m % 2][:, gi * SEQ:gi * SEQ + nk], bk[:, 0:nk])
                        freed(("pt", m, gi), i, s_pT if gi == len(heads(u)) - 1 else None)
                if n % 3 == 0 and 3 <= n <= 18:
                    stage(n // 3 + 1)
                if n in (14, 19, 24):
                    state_copies((14, 19, 24).index(n) + 1)

            for part, (s_, at) in enumerate([(s_u, 2), (s_u, 6), (s_mix, 1), (s_mix, 3), (s_mix, 5), (s_mix, 7)]):
                act.wait_ge(s_, at)
                state_copies(4 + part)
            act.wait_ge(s_x1, 6)
            for h in range(2):
                bk = filled(act, ("g2", h))
                i = copy(g2p[:, h * 512:(h + 1) * 512], bk[:, :])
                freed(("g2", h), i, s_g2)
                bk = filled(act, ("g2s", h))
                i = copy(g2s[:, h * 512:(h + 1) * 512], bk[0:NB, :])
                freed(("g2s", h), i, s_g2)

            root(2)
            root(3)
            for t in range(2):
                for h in range(2):
                    bk = filled(act, ("nT", t, h))
                    for j in range(4):
                        k = 4 * h + j
                        i = A(hT3[:, k, t * P:(t + 1) * P], bk[:, j * P:(j + 1) * P], ACT.Identity,
                              bias=mod[:, 24 + k, NB:NB + 1], scale=mod[:, 32 + k, NB:NB + 1])
                    freed(("nT", t, h), i, s_h2T if h else None)
            for t, (t0, tn) in enumerate(TT):
                for h in range(2):
                    bk = filled(act, ("h2", t, h))
                    i = copy(h2[0:tn, t, h * 512:(h + 1) * 512], bk[0:tn, :])
                    freed(("h2", t, h), i, s_h2)
            act.wait_ge(s_rlg, 1)
            A(work[:, 400:412], work[:, 400:412], ACT.Exp).then_inc(s_rexp, 1)
            act.wait_ge(s_rlg, 2)
            A(work[:, 420:423], work[:, 420:423], ACT.Exp).then_inc(s_rexp, 1)

            act.wait_ge(s_round, 2)
            n_r = act.value_load(rounds_i[0:1, 0:1], min_val=1, max_val=MAXR)
            def tokens_T(nth):
                act.wait_ge(s_xgT, nth)
                copy(gates[:, 512:1024], bank[1][:, :]).then_inc(s_xT, 1)

            tokens_T(1)
            act.sem_inc(s_yrow, 1)
            with act.Fori(0, n_r * (NE // UNR)) as i4:
                for u in range(UNR):
                    n = UNR * i4 + u + 1
                    act.wait_ge(s_gu, n)
                    A(sg, bank[2][:, 0:256], ACT.Silu).then_inc(s_sg, 1)
                    tokens_T(n + 1)
                    act.wait_ge(s_yt, n)
                    act.wait_ge(s_yst[u], 16 * i4 + 16)
                    copy(yrow[u], bank[4][:, :]).then_inc(s_yrow, 1)
            root(4)
            act.wait_ge(s_st, 16 * (3 * NB + 3))
            act.wait_ge(s_vout, 16 * 10)
            act.wait_ge(s_kout[0], 16 * 8)
            act.wait_ge(s_kout[1], 16 * 4)

        @block.vector
        def _(dve):
            V = nc.vector
            link = chain(dve, s_dve)

            def freed(key, ins, also=None):
                b, n = turn[key]
                ins.then_inc(free[b], 1)
                if also is not None:
                    dve.wait_ge(free[b], n + 1)
                    dve.sem_inc(also, 1)

            def normalize(rows, signal=None, affine=False):
                for t, (src, _, tn) in enumerate(rows):
                    link(V.bn_stats(stat[0:tn, 4:10], src[:, 0:512]))
                    link(V.bn_stats(stat[0:tn, 10:16], src[:, 512:DM]))
                    link(V.bn_aggr(nst[0:tn, t, :], stat[0:tn, 4:16]))
                V.tensor_scalar(sdev[:, :], nst[:, :, 1], EPS, None, ALU.add).then_inc(s_var, 1)
                norms[0] += 1
                dve.wait_ge(s_sd, norms[0])
                link(V.reciprocal(sdev[:, :], sdev[:, :]))
                for t, (src, dst, tn) in enumerate(rows):
                    if affine:
                        link(V.scalar_tensor_tensor(dst, src, nst[0:tn, t, 0:1], lng[0:tn, :], ALU.subtract, ALU.mult))
                        i = V.scalar_tensor_tensor(dst, dst, sdev[0:tn, t:t + 1], lnb[0:tn, :], ALU.mult, ALU.add)
                        if signal is None:
                            link(i)
                        else:
                            i.then_inc(signal, 1)
                        continue
                    i = V.tensor_scalar(dst, src, nst[0:tn, t, 0:1], sdev[0:tn, t:t + 1], ALU.subtract, ALU.mult)
                    if signal is None:
                        link(i)
                    else:
                        i.then_inc(signal, 1)

            norms = [0]
            link(V.memset(nst[:, :, :], 1.0))
            dve.wait_ge(s_x, 48)
            normalize([(x[0:tn, t, :], x[0:tn, t, :], tn) for t, (t0, tn) in enumerate(TT)], s_norm)

            dve.wait_ge(s_cst, 16)
            with dve.Fori(0, NB // 4) as i2:
                for bb in range(4):
                    dve.wait_ge(s_qbc, 4 * i2 + bb + 1)
                    for hh in range(2):
                        kt = ring[:, 4 + hh, :]
                        n = 8 * i2 + 2 * bb + hh
                        dve.wait_ge(w_full[4 + hh], i2 * (4 * 16 * HPG) + (bb + 1) * 16 * HPG)
                        k3 = kt.rearrange("p (k n) -> p k n", k=HPG)
                        V.tensor_tensor(k3, k3, qbc[:, bb * AW:(bb + 1) * AW].unsqueeze(1).to_broadcast([P, HPG, AW]),
                                        ALU.mult).then_inc(s_kmul, 1)
                        dve.wait_ge(s_kmul, n + 1)
                        V.tensor_reduce(S[:, bass.ds(n * (HPG * HA), HPG * HA)],
                                        kt.rearrange("p (m d) -> p m d", d=HD), AX.X, ALU.add).then_inc(s_kred, 1)
            for g in range(NG):
                kt = landed(dve, ("kd", g))[:, 0:2048]
                dve.wait_ge(s_qbc, NB + (g + 1) * NB)
                V.tensor_tensor(kt, kt, qbc[:, 0:2048], ALU.mult).then_inc(s_kdmul, 1)
                dve.wait_ge(s_kdmul, g + 1)
                i = V.tensor_reduce(Sd4[:, :, g, :], kt.rearrange("p (b h d) -> p b h d", b=NB, h=HB), AX.X, ALU.add)
                i.then_inc(s_kdred, 1)

            bsm = work[0:NB, 0:1024]
            i8 = ident[0:NB, 0:NB]
            dve.wait_ge(s_kout[0], 8 * 16)
            dve.wait_ge(s_kout[1], 4 * 16)
            for h in range(2):
                bk = filled(dve, ("bs", h))
                i = V.tensor_tensor(bsm[:, h * 512:(h + 1) * 512].rearrange("p (b n) -> p b n", b=4),
                                    bk[0:NB, :].rearrange("p (b n) -> p b n", b=4),
                                    i8[:, 4 * h:4 * h + 4].unsqueeze(2).to_broadcast([NB, 4, P]), ALU.mult)
                freed(("bs", h), i)
            dve.wait_ge(free[4], turn[("bs", 0)][1] + 1)
            dve.wait_ge(free[5], turn[("bs", 1)][1] + 1)
            pgs = work[0:NB, 1024:1152]
            link(V.tensor_reduce(pgs, bsm.rearrange("p (b n) -> p n b", b=NB), AX.X, ALU.add))
            bs = work[0:NB, 1152:1216]
            link(V.tensor_reduce(bs.rearrange("p (k h) -> p k h", k=NBLK),
                                 pgs.rearrange("p (k t h) -> p k h t", k=NBLK, t=2), AX.X, ALU.add))
            bsh = bs.rearrange("p (k h) -> p h k", k=NBLK)
            gt = work[0:NB, 1216:1728].rearrange("p (h i j) -> p h i j", h=HA, i=NBLK)
            eq = work[0:NB, 0:512].rearrange("p (h i j) -> p h i j", h=HA, i=NBLK)
            sj = bsh.unsqueeze(2).to_broadcast([NB, HA, NBLK, NBLK])
            si = bsh.unsqueeze(3).to_broadcast([NB, HA, NBLK, NBLK])
            link(V.tensor_tensor(gt, sj, si, ALU.is_gt))
            link(V.tensor_tensor(eq, sj, si, ALU.is_equal))
            tie8 = tie[0:NB, :].unsqueeze(1).to_broadcast([NB, HA, 64])
            link(V.tensor_tensor(eq.rearrange("p h i j -> p h (i j)"), eq.rearrange("p h i j -> p h (i j)"), tie8, ALU.mult))
            link(V.tensor_tensor(gt.rearrange("p h i j -> p (h i j)"), gt.rearrange("p h i j -> p (h i j)"),
                                 eq.rearrange("p h i j -> p (h i j)"), ALU.add))
            rank = work[0:NB, 512:576]
            link(V.tensor_reduce(rank.rearrange("p (h k) -> p h k", h=HA), gt, AX.X, ALU.add))
            pen = work[0:NB, 576:640]
            link(V.tensor_scalar(pen.rearrange("p (k h) -> p h k", k=NBLK), rank.rearrange("p (h k) -> p h k", h=HA),
                                 TOPK - 0.5, NEG, ALU.is_gt, ALU.mult))
            penD = work[0:NB, 2048:2560].rearrange("p (b n) -> p b n", b=NB)
            i8b = i8.unsqueeze(2).to_broadcast([NB, NB, 64])
            V.tensor_tensor(penD, i8b, pen.unsqueeze(1).to_broadcast([NB, NB, 64]), ALU.mult).then_inc(s_pen, 1)

            dve.wait_ge(s_sbias, 1)
            S3 = S[:, :].rearrange("p (b n) -> p b n", b=NB)
            link(V.tensor_tensor(S3, S3, sbias[:, 0:P].unsqueeze(1).to_broadcast([P, NB, P]), ALU.add))
            Sd3 = Sd[:, :].rearrange("p (b n) -> p b n", b=NB)
            link(V.tensor_tensor(Sd3, Sd3, sbias[:, P:P + NG * HB].unsqueeze(1).to_broadcast([P, NB, NG * HB]), ALU.add))
            bk = filled(dve, "pen")
            Sb = S[:, :].rearrange("p (q t h) -> p q t h", t=2, h=HA)
            i = V.tensor_tensor(Sb, Sb, bk[:, :].rearrange("p (q h) -> p q h", h=HA).unsqueeze(2).to_broadcast([P, NB * NBLK, 2, HA]), ALU.add)
            freed("pen", i)
            dve.wait_ge(free[4], turn["pen"][1] + 1)
            m3 = m12[:, :].rearrange("p (b h) -> p b h", b=NB)
            link(V.tensor_reduce(m3[:, :, 0:HA], S4.rearrange("p b k h -> p b h k"), AX.X, ALU.max))
            V.tensor_reduce(m3[:, :, HA:HS], Sd4.rearrange("p b g h -> p b h g"), AX.X, ALU.max).then_inc(s_m12, 1)
            dve.wait_ge(s_own, 1)
            ownl = own[:, 40:60]
            link(V.tensor_scalar(own[:, 0:HALL], own[:, 0:HALL], QSCALE, None, ALU.mult))
            link(V.tensor_tensor(ownl, own[:, 0:HALL], own[:, HALL:2 * HALL], ALU.add))
            o12 = own[:, 0:HS]
            link(V.tensor_copy(o12[:, 0:HA], ownl[:, 0:HA]))
            link(V.tensor_reduce(o12[:, HA:HS], ownl[:, HA:HALL].rearrange("p (g h) -> p h g", g=NG), AX.X, ALU.max))
            i8c = i8.unsqueeze(2).to_broadcast([NB, NB, HS])
            ownD3 = ownD[:, :].rearrange("p (b h) -> p b h", b=NB)
            V.tensor_tensor(ownD3, i8c, o12.unsqueeze(1).to_broadcast([NB, NB, HS]), ALU.mult).then_inc(s_ownx, 1)
            bk = filled(dve, "mxT")
            mrow = st96[0:96, 110:111]
            i = V.tensor_reduce(mrow, bk[0:96, 0:P], AX.X, ALU.max)
            freed("mxT", i)
            dve.wait_ge(free[5], turn["mxT"][1] + 1)
            bk = filled(dve, "ownx")
            i = V.tensor_tensor(mrow, mrow, bk[0:96, 0:1], ALU.max)
            freed("ownx", i)
            dve.wait_ge(free[4], turn["ownx"][1] + 1)
            link(V.tensor_scalar(mrow, mrow, -1.0, None, ALU.mult))
            link(V.tensor_scalar(st96[0:96, 0:96], ident[0:96, 0:96], mrow, None, ALU.mult))
            V.tensor_scalar(st96[0:96, 96:96 + HS], h96, mrow, None, ALU.mult).then_inc(s_negm, 1)
            bk = filled(dve, "negm")
            nm = bk[:, 0:96].rearrange("p (b h) -> p b h", b=NB)
            V.tensor_tensor(S4, S4, nm[:, :, 0:HA].unsqueeze(2).to_broadcast([P, NB, NPG, HA]), ALU.add)
            V.tensor_tensor(Sd4, Sd4, nm[:, :, HA:HS].unsqueeze(2).to_broadcast([P, NB, NG, HB]), ALU.add)
            V.tensor_tensor(ownl[:, 0:HA], ownl[:, 0:HA], bk[0:NB, 96:96 + HA], ALU.add)
            i = V.tensor_tensor(ownl[:, HA:HALL].rearrange("p (g h) -> p g h", g=NG),
                                ownl[:, HA:HALL].rearrange("p (g h) -> p g h", g=NG),
                                bk[0:NB, 96 + HA:96 + HS].unsqueeze(1).to_broadcast([NB, NG, HB]), ALU.add)
            freed("negm", i, s_sub)
            dve.wait_ge(s_exp, 3)
            link(V.tensor_reduce(m3[:, :, 0:HA], S4.rearrange("p b k h -> p b h k"), AX.X, ALU.add))
            link(V.tensor_reduce(m3[:, :, HA:HS], Sd4.rearrange("p b g h -> p b h g"), AX.X, ALU.add))
            link(V.tensor_copy(o12[:, 0:HA], ownl[:, 0:HA]))
            link(V.tensor_reduce(o12[:, HA:HS], ownl[:, HA:HALL].rearrange("p (g h) -> p h g", g=NG), AX.X, ALU.add))
            V.tensor_tensor(ownD3, i8c, o12.unsqueeze(1).to_broadcast([NB, NB, HS]), ALU.mult).then_inc(s_sum, 1)
            V.tensor_tensor(powD[:, 0:NB * HA].rearrange("p (b h) -> p b h", b=NB), i8.unsqueeze(2).to_broadcast([NB, NB, HA]),
                            ownl[:, 0:HA].unsqueeze(1).to_broadcast([NB, NB, HA]), ALU.mult)
            link(V.tensor_tensor(powD[:, NB * HA:].rearrange("p (b h) -> p b h", b=NB), i8c,
                                 ownl[:, HA:HALL].unsqueeze(1).to_broadcast([NB, NB, NG * HB]), ALU.mult))
            link(V.tensor_copy(work[0:96, 2560:2688].rearrange("p (r h) -> p r h", h=HA),
                               h96[:, 0:HA].unsqueeze(1).to_broadcast([96, P // HA, HA])))
            bk = filled(dve, "sum")
            i = V.reciprocal(mrow, bk[0:96, 0:1])
            freed("sum", i)
            dve.wait_ge(free[4], turn["sum"][1] + 1)
            V.tensor_scalar(st96[0:96, 0:NB], e96, mrow, None, ALU.mult).then_inc(s_rec, 1)
            bk = filled(dve, "rs")
            V.tensor_copy(rinv[:, 0:NB], bk[:, 0:NB])
            i = V.tensor_copy(rinv[0:HB, NB:2 * NB], bk[0:HB, NB:2 * NB])
            freed("rs", i, s_rs)

            def logits(n):
                u = units[n]
                nk = P * (u[2] + 1)
                if n >= 2:
                    dve.wait_ge(s_pT, n - 1)
                if n == 0:
                    dve.wait_ge(s_toea, 16)
                if u[0] == "b" and n == 2 * HA:
                    dve.wait_ge(s_toeb, 16)
                hh = heads(u)
                for gi in range(len(hh)):
                    row = toe_a[:, u[1], nk - 1:nk] if u[0] == "a" else toe_b[:, gi * HB + u[1], nk - 1:nk]
                    bias = bass.AP(row.tensor, row.offset, [list(row.ap[0]), [-1, nk]])
                    bk = filled(dve, ("sc", n, gi))
                    i = V.scalar_tensor_tensor(pk[n % 2][:, gi * nk:(gi + 1) * nk], bk[:, 0:nk], QSCALE, bias,
                                               ALU.mult, ALU.add)
                    freed(("sc", n, gi), i)
                b, nt = turn[("sc", n, len(hh) - 1)]
                dve.wait_ge(free[b], nt + 1)
                V.tensor_reduce(stat[:, n % 2:n % 2 + 1], pk[n % 2][:, 0:len(hh) * nk], AX.X, ALU.max, negate=True).then_inc(s_lg, 1)

            def norm(n):
                u = units[n]
                w = len(heads(u)) * P * (u[2] + 1)
                dve.wait_ge(s_pexp, n + 1)
                r = stat[:, 20 + n % 2:21 + n % 2]
                link(V.reciprocal(r, stat[:, 2 + n % 2:3 + n % 2]))
                V.tensor_scalar(pk[n % 2][:, 0:w], pk[n % 2][:, 0:w], r, None, ALU.mult).then_inc(s_pn, 1)

            def output(n):
                u = units[n]
                par = u[1] % 2
                row = (0 if u[0] == "a" else 4) + u[1] // 2
                bk = filled(dve, ("po", n))
                i = V.tensor_copy(oT3[par * HD:(par + 1) * HD, row, u[2] * P:(u[2] + 1) * P], bk[par * HD:(par + 1) * HD, 0:P])
                freed(("po", n), i, s_po)

            for n in range(len(units) + 3):
                if n < len(units):
                    logits(n)
                if 1 <= n <= len(units):
                    norm(n - 1)
                if n >= 3:
                    output(n - 3)
                if n % 3 == 0 and 3 <= n <= len(units):
                    b = n // 3 - 1
                    bk = filled(dve, ("ov", b))
                    freed(("ov", b), V.tensor_tensor(vm[b % 2], bk[:, :], blkdiag, ALU.mult), s_vm)
                if n % 3 == 2 and n >= 5:
                    b = n // 3 - 1
                    bk = filled(dve, ("vt", b))
                    freed(("vt", b), V.tensor_copy(oT3[:, 0:4, SEQ + b:SEQ + b + 1], bk[:, 0:4].unsqueeze(2)), s_oa)
            for b in range(NB):
                bk = filled(dve, ("od", b))
                if b >= 2:
                    dve.wait_ge(s_odt, b - 1)
                i = V.tensor_tensor(odm[b % 2], bk[0:HB, 0:256], blkdiag[0:HB, 0:256], ALU.mult)
                freed(("od", b), i, s_vm)
            bk = filled(dve, "odT")
            i = V.tensor_copy(oT3[:, 4:6, SEQ:NT], bk[:, 0:2 * NB].rearrange("p (c b) -> p c b", c=2))
            freed("odT", i, s_oa)

            t1, t2 = work[:, 0:NT], work[:, 512:512 + NT]
            for j in range(KC):
                bk = filled(dve, ("ya", j))
                i = V.tensor_tensor(t1, bk[:, 0:NT], gates3[:, j, :], ALU.mult)
                freed(("ya", j), i)
                bk = filled(dve, ("yb", j))
                i = V.tensor_tensor(t2, bk[:, 0:NT], gates3[:, 8 + j, :], ALU.mult)
                freed(("yb", j), i)
                dve.wait_ge(free[turn[("yb", j)][0]], turn[("yb", j)][1] + 1)
                i = V.tensor_tensor(hT3[:, j, :], t1, t2, ALU.add)
                i.then_inc(s_u, 1)
                dve.wait_ge(s_u, j + 1)
            for j in range(KC):
                bk = filled(dve, ("mix", j))
                V.tensor_scalar(mixT[:, j, 0:SEQ], bk[:, 0:SEQ], mod[:, 16 + j, NB:NB + 1], None, ALU.mult)
                i = V.tensor_tensor(mixT[:, j, SEQ:NT], bk[:, SEQ:NT], mod[:, 16 + j, 0:NB], ALU.mult)
                freed(("mix", j), i, s_mix)

            dve.wait_ge(s_x2, 48)
            for t, (t0, tn) in enumerate(TT):
                for h in range(2):
                    c = slice(h * 512, (h + 1) * 512)
                    bk = filled(dve, ("mt", t, h))
                    i = V.scalar_tensor_tensor(x[0:tn, t, c], x[0:tn, t, c], ALPHA, bk[0:tn, :], ALU.mult, ALU.add)
                    freed(("mt", t, h), i, s_x1)
            dve.wait_ge(s_x1, 6)
            dve.wait_ge(s_ln1, 32)
            dve.wait_ge(s_vout, 10 * 16)
            normalize([(x[0:tn, t, :], x[0:tn, t, :], tn) for t, (t0, tn) in enumerate(TT)], affine=True)
            normalize([(x[0:tn, t, :], h2[0:tn, t, :], tn) for t, (t0, tn) in enumerate(TT)], s_n2)
            for h in range(2):
                bk = filled(dve, ("nT", 2, h))
                hv = hT3[:, 4 * h:4 * h + 4, SEQ:NT]
                i = V.tensor_tensor(hv, bk[:, :].rearrange("p (k n) -> p k n", k=4)[:, :, 0:NB],
                                    mod[:, 32 + 4 * h:36 + 4 * h, 0:NB], ALU.mult)
                freed(("nT", 2, h), i)
                dve.wait_ge(free[4 + h], turn[("nT", 2, h)][1] + 1)
                i = V.tensor_tensor(hv, hv, mod[:, 24 + 4 * h:28 + 4 * h, 0:NB], ALU.add)
                link(i)
            V.memset(work[:, 0:512], 0.0).then_inc(s_h2T, 1)

            lg = work[:, 112:220].rearrange("p (t n) -> p t n", t=3)
            dve.wait_ge(s_h2T, 3)
            dve.wait_ge(s_rb, 32)
            rb = work[:, 2600:2636]
            bk = filled(dve, "lg")
            link(V.tensor_tensor(lg[:, 0:2, :], bk[:, 0:72].rearrange("p (t n) -> p t n", t=2),
                                 rb.unsqueeze(1).to_broadcast([P, 2, 36]), ALU.add))
            i = V.tensor_tensor(lg[0:NB, 2, :], bk[0:NB, 72:108], rb[0:NB, :], ALU.add)
            freed("lg", i)
            dve.wait_ge(free[2], turn["lg"][1] + 1)
            lgg = lg[:, :, 0:NGRP]
            lge = lg[:, :, NGRP:36]

            def rank_of(out, s3, n, a, b):
                A_ = work[:, a:a + 3 * n * n].rearrange("p (t i j) -> p t i j", t=3, i=n)
                B_ = work[:, b:b + 3 * n * n].rearrange("p (t i j) -> p t i j", t=3, i=n)
                j_ = s3.unsqueeze(2).to_broadcast([P, 3, n, n])
                i_ = s3.unsqueeze(3).to_broadcast([P, 3, n, n])
                link(V.tensor_tensor(A_, j_, i_, ALU.is_gt))
                link(V.tensor_tensor(B_, j_, i_, ALU.is_equal))
                tt = tie.rearrange("p (i j) -> p i j", i=8)[:, 0:n, 0:n].unsqueeze(1).to_broadcast([P, 3, n, n])
                link(V.tensor_tensor(B_, B_, tt, ALU.mult))
                link(V.tensor_tensor(A_, A_, B_, ALU.add))
                link(V.tensor_reduce(out, A_, AX.X, ALU.add))

            rk4 = work[:, 230:242].rearrange("p (t n) -> p t n", t=3)
            ohg = work[:, 242:254].rearrange("p (t n) -> p t n", t=3)
            gm = work[:, 254:257]
            ex = work[:, 400:412].rearrange("p (t n) -> p t n", t=3)
            rank_of(rk4, lgg, NGRP, 600, 700)
            link(V.tensor_scalar(ohg, rk4, 0.0, None, ALU.is_equal))
            link(V.tensor_reduce(gm, lgg, AX.X, ALU.max))
            V.tensor_tensor(ex, lgg, gm.unsqueeze(2).to_broadcast([P, 3, NGRP]), ALU.subtract).then_inc(s_rlg, 1)
            les = work[:, 260:284].rearrange("p (t e) -> p t e", t=3)
            tmp4 = work[:, 800:896].rearrange("p (t e g) -> p t e g", t=3, g=NGRP)
            for t in range(3):
                link(V.tensor_tensor(tmp4[:, t], lge[:, t, :].rearrange("p (g e) -> p e g", g=NGRP),
                                     ohg[:, t, :].unsqueeze(1).to_broadcast([P, EG, NGRP]), ALU.mult))
            link(V.tensor_reduce(les, tmp4, AX.X, ALU.add))
            rk8 = work[:, 290:314].rearrange("p (t e) -> p t e", t=3)
            rank_of(rk8, les, EG, 1000, 1200)
            oh = [work[:, 320 + 24 * i:344 + 24 * i].rearrange("p (t e) -> p t e", t=3) for i in range(2)]
            vv = [work[:, 370 + 3 * i:373 + 3 * i] for i in range(2)]
            tm = work[:, 1400:1424].rearrange("p (t e) -> p t e", t=3)
            for i_ in range(2):
                link(V.tensor_scalar(oh[i_], rk8, float(i_), None, ALU.is_equal))
                link(V.tensor_tensor(tm, oh[i_], les, ALU.mult))
                link(V.tensor_reduce(vv[i_], tm, AX.X, ALU.add))
            V.tensor_tensor(work[:, 420:423], vv[1], vv[0], ALU.subtract).then_inc(s_rlg, 1)
            ohe = [work[:, 1500 + 96 * i:1596 + 96 * i].rearrange("p (t g e) -> p t g e", t=3, g=NGRP) for i in range(2)]
            for i_ in range(2):
                for t in range(3):
                    link(V.tensor_tensor(ohe[i_][:, t], ohg[:, t, :].unsqueeze(2).to_broadcast([P, NGRP, EG]),
                                         oh[i_][:, t, :].unsqueeze(1).to_broadcast([P, NGRP, EG]), ALU.mult))
            M = work[:, 0:96]
            V.tensor_tensor(M, work[:, 1500:1596], work[:, 1596:1692], ALU.add).then_inc(s_mask, 1)
            dve.wait_ge(s_rexp, 2)
            sm4, e2, den = work[:, 430:433], work[:, 420:423], work[:, 436:439]
            link(V.tensor_reduce(sm4, ex, AX.X, ALU.add))
            link(V.tensor_scalar(den, e2, 1.0, None, ALU.add))
            link(V.tensor_tensor(den, den, sm4, ALU.mult))
            link(V.reciprocal(den, den))
            link(V.tensor_copy(wts[:, :, 0], den))
            link(V.tensor_tensor(wts[:, :, 1], den, e2, ALU.mult))
            pos = work[:, 1700:1796]
            link(V.memset(pos, 0.0))
            bk = filled(dve, "pos")
            link(V.tensor_copy(pos[:, 0:64], bk[:, 0:64]))
            link(V.tensor_copy(pos[0:NB, 64:96], bk[0:NB, 64:96]))
            mc = work[0:1, 440:441]
            i = V.tensor_reduce(mc, bk[0:1, 96:128], AX.X, ALU.max)
            freed("pos", i)
            dve.wait_ge(free[3], turn["pos"][1] + 1)
            rr = work[0:1, 442:443]
            link(V.tensor_scalar(rr, mc, float(SLOT), 1.0, ALU.is_gt, ALU.add))
            for r in range(2, MAXR):
                link(V.tensor_scalar(work[0:1, 444:445], mc, float(r * SLOT), None, ALU.is_gt))
                link(V.tensor_tensor(rr, rr, work[0:1, 444:445], ALU.add))
            V.tensor_copy(rounds_i[:, :], rr).then_inc(s_round, 1)
            pm = work[:, 1800:1896]
            link(V.tensor_scalar(pm, pos, 1.0, None, ALU.add))
            link(V.tensor_tensor(pm, pm, M, ALU.mult))
            link(V.memset(posx[:, :, MAXR * NE:], -1.0))
            for r in range(MAXR):
                i = V.tensor_scalar(posx[:, :, r * NE:(r + 1) * NE], pm.rearrange("p (t e) -> p t e", t=3),
                                    -1.0 - SLOT * r, None, ALU.add)
                link(i)

            def places(s, n):
                V.tensor_copy(rowf[:, s, 0:3], rowx[:, :, bass.ds(n, 1)].rearrange("p t o -> p (t o)"))
                for t in range(3):
                    i = V.tensor_scalar(G[s][:, t, :], iota, posx[:, t, bass.ds(n, 1)], None, ALU.is_equal)
                i.then_inc(s_G, 1)

            tok = cst[:, C_TOK:C_TOK + 3]
            ohe2 = work[:, 1596:1692].rearrange("p (t e) -> p t e", t=3)
            rx = rowx[:, :, 0:NE]
            link(V.tensor_scalar(rx, ohe2, float(2 * NT), None, ALU.mult))
            link(V.tensor_tensor(rx, rx, tok.unsqueeze(2).to_broadcast([P, 3, NE]), ALU.add))
            for r in range(1, MAXR):
                link(V.tensor_copy(rowx[:, :, r * NE:(r + 1) * NE], rx))
            link(V.memset(rowx[:, :, MAXR * NE:], 0.0))
            dve.wait_ge(s_h2, 6)
            dve.wait_ge(s_round, 1)
            n_r = dve.value_load(rounds_i[0:1, 0:1], min_val=1, max_val=MAXR)

            def tokens_out(nth):
                dve.wait_ge(s_xg, nth)
                V.tensor_copy(xg, bank[0][:, :]).then_inc(s_xgs, 1)

            def rows_out(u, nth, stored):
                V.tensor_scalar(stat[:, 23:24], bank[5][:, 0:1], 0.5, 1e6, ALU.is_lt, ALU.mult).then_inc(s_big, 1)
                dve.wait_ge(s_yst[u], stored)
                dve.wait_ge(s_big, nth)
                V.scalar_tensor_tensor(ridx[:, u:u + 1], bank[5][:, 0:1], cst[:, C_HM1:C_HM1 + 1], stat[:, 23:24],
                                       ALU.add, ALU.max).then_inc(s_idx, 1)

            dve.sem_inc(s_idx, 1)
            places(0, 0)
            places(1, 1)
            dve.sem_inc(s_round, 1)
            for m in range(2):
                tokens_out(m + 1)
                places(m, m + 2)
                rows_out(m, m + 1, 16)
            with dve.Fori(0, n_r * (NE // UNR)) as i4:
                for u in range(UNR):
                    n = UNR * i4 + u + 1
                    dve.wait_ge(s_sg, n)
                    V.tensor_tensor(act_g, sg, bank[2][:, 256:512], ALU.mult).then_inc(s_act, 1)
                    dve.wait_ge(s_aTp, n)
                    V.tensor_copy(aT, bank[3][:, 0:256]).then_inc(s_aT, 1)
                    tokens_out(n + 2)
                    places(u % 2, n + 3)
                    rows_out((u + 2) % UNR, n + 2, 16 * i4 + 16 * ((u + 2) // UNR + 1))

            for u in range(UNR):
                dve.wait_ge(s_yst[u], 16)
            dve.wait_ge(s_g2, 4)
            for t, (t0, tn) in enumerate(TT):
                ya, yb = ring[0:tn, t, 0:DM], ring[0:tn, t, DM:2 * DM]
                xt = x[0:tn, t, :]
                dve.wait_ge(s_gat[t], 32)
                link(V.tensor_scalar(ya, ya, wts[0:tn, t, 0:1], None, ALU.mult))
                link(V.scalar_tensor_tensor(ya, yb, wts[0:tn, t, 1:2], ya, ALU.mult, ALU.add))
                link(V.tensor_tensor(ya, ya, g2p[0:tn, :] if t < 2 else g2s, ALU.mult))
                link(V.scalar_tensor_tensor(xt, xt, ALPHA, ya, ALU.mult, ALU.add))
            normalize([(x[0:tn, t, :], x[0:tn, t, :], tn) for t, (t0, tn) in enumerate(TT)], s_y, affine=True)

        @block.gpsimd
        def _(pool):
            def load_w(name):
                at = weights.index(name)
                if at >= 4:
                    filled(pool, last_use[weights[at - 4]])
                dst = ring[:, slot_of(name), :]
                kind, t = name
                if kind == "ada":
                    src = w_ada[0].rearrange("(k p) n -> p k n", p=P)[:, :, t * 512:(t + 1) * 512]
                elif kind == "win":
                    w = 512 if t < 11 else 256
                    src = w_in[0].rearrange("(k p) n -> p k n", p=P)[:, :, t * 512:t * 512 + w]
                elif kind == "wo":
                    src = w_out[0].rearrange("(k p) n -> p k n", p=P)[:, :, t * 512:(t + 1) * 512]
                else:
                    src = (w_proj_a if kind == "wpa" else w_proj_b)[0].rearrange("(k p) n -> p k n", p=P)
                n = src.shape[1] * src.shape[2]
                pool.dma_start(dst[:, 0:n].rearrange("p (k n) -> p k n", k=src.shape[1]), src)\
                    .then_inc(w_full[slot_of(name)], 16)

            nc.gpsimd.memset(cT[:, KC * (NB + 1):], 0.0).then_inc(s_cT, 1)
            for name in weights[0:4]:
                load_w(name)
            pool.wait_ge(s_bt, 17)
            nc.gpsimd.tensor_scalar(bT[:, 8:16], bT[:, 8:16], 1.0, None, ALU.add)
            nc.gpsimd.tensor_scalar(bT[:, 32:40], bT[:, 32:40], 1.0, None, ALU.add).then_inc(s_bT, 1)
            for name in weights[4:8]:
                load_w(name)
            pool.wait_ge(s_hs, 1)
            hs3 = hs[:, :].rearrange("p (k n) -> p k n", k=KC)
            nc.gpsimd.tensor_tensor(hs3, hs3, mod[:, 8:16, 0:NB], ALU.mult).then_inc(s_pool, 1)
            pool.wait_ge(s_pool, 1)
            nc.gpsimd.tensor_tensor(hT3[:, :, SEQ:NT], hs3, mod[:, 0:8, 0:NB], ALU.add).then_inc(s_hTs, 1)
            pool.wait_ge(s_toev, 4)
            pool.dma_start(toe_d[0:HA * VLEN].rearrange("(h w) -> h w", h=HA), toev[:, 0, :]).then_inc(s_toes, 16)
            for g in range(NG):
                a = (HA + g * HB) * VLEN
                pool.dma_start(toe_d[a:a + HB * VLEN].rearrange("(h w) -> h w", h=HB), toev[0:HB, 1 + g, :]).then_inc(s_toes, 16)
            pool.wait_ge(s_toes, 64)
            pool.wait_ge(s_hTp, 2)
            pool.wait_ge(s_hs, 1)

            def toeplitz(h0, hn):
                return bass.AP(toe_d, h0 * VLEN, [[1, P], [VLEN, hn], [1, SEQ]])

            pool.dma_start(toe_b, toeplitz(HA, NG * HB)).then_inc(s_toeb, 16)
            for name in weights[8:14]:
                load_w(name)
            pool.wait_ge(s_z, 20)
            q3 = [zT3[:, 0:4, SEQ:NT], zT3[:, 8:14, SEQ:NT]]
            k3 = [zT3[:, 4:8, SEQ:NT], zT3[:, 14:20, SEQ:NT]]
            nc.gpsimd.tensor_tensor(prod[:, 0:4 * NB].rearrange("p (c b) -> p c b", c=4), q3[0], k3[0], ALU.mult)
            nc.gpsimd.tensor_tensor(prod[:, 4 * NB:].rearrange("p (c b) -> p c b", c=6), q3[1], k3[1], ALU.mult).then_inc(s_prod, 1)
            for name in weights[14:20]:
                load_w(name)
            filled(pool, ("z", 45))
            pool.dma_start(toe_a, toeplitz(0, HA)).then_inc(s_toea, 16)
            for name in weights[20:]:
                load_w(name)
            pool.wait_ge(s_pt, 16)
            pool.wait_ge(s_kdred, 2)
            load_pages(pool, v_pages, 0, 1, s_vhi)
            with pool.Fori(1, NB) as b:
                pool.wait_ge(s_vread[1], b)
                pool.sem_inc(s_pool, 1)
                load_pages(pool, v_pages, b, 1, s_vhi)
            pool.wait_ge(s_po, len(units))
            pool.dma_start(x[:, 0:2, :], x_prompt[0].rearrange("(t p) d -> p t d", p=P)).then_inc(s_x2, 32)
            pool.dma_start(x[0:NB, 2, :], x_sample[:, 0, :]).then_inc(s_x2, 16)
            wr = work[:, 2700:2700 + KC * 36].rearrange("p (k n) -> p k n", k=KC)
            pool.dma_start(wr[:, :, 0:NGRP], w_rg[0].rearrange("(k p) n -> p k n", p=P)).then_inc(s_wr, 16)
            for g in range(NGRP):
                c = NGRP + g * EG
                pool.dma_start(wr[:, :, c:c + EG], w_re[0, g].rearrange("(k p) n -> p k n", p=P)).then_inc(s_wr, 16)
            pool.dma_start(work[:, 2600:2604], b_rg[0].partition_broadcast(P)).then_inc(s_rb, 16)
            pool.dma_start(work[:, 2604:2636], b_re[0].rearrange("g e -> (g e)").partition_broadcast(P)).then_inc(s_rb, 16)
            pool.dma_start(lng, ln1_g[0].partition_broadcast(P)).then_inc(s_ln1, 16)
            pool.dma_start(lnb, ln1_b[0].partition_broadcast(P)).then_inc(s_ln1, 16)
            pool.wait_ge(s_n2, 3)
            for u in range(UNR):
                c = slice(u % 2 * 512, u % 2 * 512 + 512)
                dst, src = ((lng, ln2_g), (lnb, ln2_b))[u // 2]
                pool.dma_start(dst[:, c], src[0, c].partition_broadcast(P)).then_inc(s_yst[u], 16)
            pool.wait_ge(s_round, 2)
            n_r = pool.value_load(rounds_i[0:1, 0:1], min_val=1, max_val=MAXR)
            with pool.Fori(0, n_r * (NE // UNR)) as i4:
                for u in range(UNR):
                    nth = pool.snap(UNR * i4 + u + 2)
                    pool.wait_ge(s_idx, nth)
                    pool.wait_ge(s_yrow, nth)
                    pool.sem_inc(s_scat, 1)
                    pool.indirect_dma_start(
                        out=ys_d[:, :], out_offset=bass.IndirectOffsetOnAxis(ap=ridx[:, u:u + 1], axis=0),
                        in_=yrow[u], in_offset=None, bounds_check=4 * NT - 1, oob_is_err=False,
                    ).then_inc(s_yst[u], 16)
            stored = pool.snap(n_r * (16 * NE // UNR) + 16)
            for u in range(UNR):
                pool.wait_ge(s_yst[u], stored)
                pool.sem_inc(s_rows, 1)

        @block.sync
        def _(sp):
            sp.dma_start(crow[0:NB, :], c_sample[:, :]).then_inc(s_c, 16)
            sp.dma_start(crow[NB:NB + 1, :], c_prompt[:, :]).then_inc(s_c, 16)
            sp.dma_start(cst[:, :], consts[:, :]).then_inc(s_cst, 16)
            sp.dma_start(brow_t, b_ada[0].rearrange("(c p) -> c p", p=P)).then_inc(s_bt, 16)
            sp.dma_start(x[:, 0:2, :], x_prompt[0].rearrange("(t p) d -> p t d", p=P)).then_inc(s_x, 32)
            sp.dma_start(x[0:NB, 2, :], x_sample[:, 0, :]).then_inc(s_x, 16)
            sp.dma_start(hot, onehots[:, :]).then_inc(s_hot, 16)
            sp.dma_start(rel[0:BUCKETS, :], rel_bias[:, :]).then_inc(s_hot, 16)
            sp.dma_start(rel[BUCKETS:BUCKETS + 1, :], negrow[:, :]).then_inc(s_hot, 16)
            sp.dma_start(pt[:, :], page_table.rearrange("(o b) n -> o (b n)", o=1)).then_inc(s_pt, 16)
            sp.wait_ge(s_pt, 16)

            def pages(cache, b, hh):
                load_pages(sp, cache, b, hh, w_full[4 + hh])

            for hh in range(2):
                pages(k_pages, 0, hh)
            with sp.Fori(1, NB) as b:
                for hh in range(2):
                    sp.wait_ge(s_kred, 2 * b + (hh - 1))
                    pages(k_pages, b, hh)

            def window(g, kv, dst):
                src = states[g][0].rearrange("b (r d) a h e -> d a r b (h e)", d=DIL[g])[0, kv]
                return dst, src

            def load_window(name, g, kv, c):
                dst = ring[:, slot_of(name), c:c + 2048].rearrange("p (b n) -> p b n", b=NB)
                dst, src = window(g, kv, dst)
                sp.dma_start(dst, src).then_inc(w_full[slot_of(name)], 16)

            for g in range(NG):
                sp.wait_ge(s_kred, 2 * NB - 1 + g) if g < 2 else sp.wait_ge(s_kdred, 1)
                load_window(("kd", g), g, 0, 0)
            sp.wait_ge(s_kdred, 3)
            pages(v_pages, 0, 0)
            with sp.Fori(1, NB) as b:
                sp.wait_ge(s_vread[0], b)
                pages(v_pages, b, 0)
            sp.wait_ge(s_vread[0], NB)
            load_window(("vd", 0), 0, 1, 0)
            load_window(("vd", 0), 1, 1, 2048)
            sp.wait_ge(s_vread[1], NB)
            load_window(("vd", 2), 2, 1, 0)

            def load_expert(s, m, e):
                w = (w_eg, w_eu, w_ed)[m]
                src = w[0, bass.ds(e, 1)].rearrange("o (k p) n -> p (o k) n", p=P)
                k = FC if m == 2 else KC
                sp.dma_start(ring[:, 3 * s + m, :].rearrange("p (k n) -> p k n", k=k), src).then_inc(ew_full[3 * s + m], 16)

            for slot in (4, 5, 0, 1, 2, 3):
                filled(sp, last_use[(("wpa", 0), ("wpb", 0), ("wo", 0), ("wo", 1), ("vd", 0), ("vd", 2))[slot]])
                load_expert(slot // 3, slot % 3, slot // 3)
            sp.wait_ge(s_round, 2)
            n_r = sp.value_load(rounds_i[0:1, 0:1], min_val=1, max_val=MAXR)
            with sp.Fori(0, n_r * (NE // 2) - 1) as m2:
                e = ((m2 + 1) % (NE // 2)) * 2
                for s in range(2):
                    sp.wait_ge(s_gu, 2 * m2 + s + 1)
                    load_expert(s, 0, e + s)
                    load_expert(s, 1, e + s)
                    sp.wait_ge(s_yt, 2 * m2 + s + 1)
                    load_expert(s, 2, e + s)
            sp.wait_ge(s_rows, UNR)
            for t, (t0, tn) in enumerate(TT):
                for i_ in range(2):
                    r = 2 * (i_ * NT + t0)
                    sp.dma_start(ring[0:tn, t, i_ * DM:(i_ + 1) * DM].rearrange("p (h n) -> p h n", h=2),
                                 ys_d[r:r + 2 * tn, :].rearrange("(p h) n -> p h n", h=2)).then_inc(s_gat[t], 16)
            for t, (t0, tn) in enumerate(TT):
                sp.wait_ge(s_y, t + 1)
                dst = y_prompt[0, t0:t0 + tn, :] if t < 2 else y_sample[:, 0, :]
                sp.dma_start(dst, x[0:tn, t, :]).then_inc(s_out, 16)
            sp.wait_ge(s_out, 48)


_INS = ["x_prompt", "x_sample", "cache_k_pages", "cache_v_pages", "page_table", "state_dil1_kv",
        "state_dil4_kv", "state_dil16_kv", "c_prompt", "c_sample", "rel_bias", "w_ada", "b_ada", "w_in",
        "w_proj_a", "w_proj_b", "w_out", "ln1_g", "ln1_b", "w_router_g", "b_router_g", "w_router_e",
        "b_router_e", "w_exp_gate", "w_exp_up", "w_exp_down", "ln2_g", "ln2_b"]
_OUTS = [(1, SEQ, DM), (NB, 1, DM), (1, 1, SEQ, HA, HD), (1, 1, SEQ, HA, HD), (1, NB, 1, HA, HD),
         (1, NB, 1, HA, HD), (1, 1, 128, 2, HB, HD), (1, NB, 128, 2, HB, HD), (1, 1, SEQ, 2, HB, HD),
         (1, NB, 512, 2, HB, HD), (1, 1, SEQ, 2, HB, HD), (1, NB, 2048, 2, HB, HD)]


def _bucket(dist):
    import numpy as np
    n = np.maximum(dist, 0)
    nf = np.maximum(n, 1).astype(np.float32)
    large = 16 + (np.log(nf / np.float32(16)) / np.float32(np.log(8.0)) * np.float32(16)).astype(np.int32)
    return np.where(n < 16, n, np.minimum(large, BUCKETS - 1))


def _constants():
    import numpy as np
    c = np.zeros((P, C_END), np.float32)
    c[:, C_ID:C_ID + P] = np.eye(P)
    c[:, C_TRI:C_TRI + P] = np.triu(np.ones((P, P)), 1)
    c[:, C_ONE:C_ONE + P] = 1
    c[:, C_IOTA:C_IOTA + SLOT] = np.arange(SLOT)
    c[:, C_IE:C_IE + NE] = np.arange(NE) * SLOT
    r = np.arange(96)
    c[r, C_E96 + r // HS] = 1
    c[r, C_H96 + r % HS] = 1
    for j in range(4):
        for h in range(HA):
            c[40 * j + h, C_BD + h * HD:C_BD + (h + 1) * HD] = 1
    i, j = np.meshgrid(np.arange(8), np.arange(8), indexing="ij")
    c[:, C_TIE:C_TIE + 64] = (j < i).reshape(-1)
    c[0:64, C_HIND] = 1
    c[64:, C_HIND + 1] = 1
    c[:, C_TOK:C_TOK + 3] = 1 + 2 * (np.arange(3)[None, :] * P + np.arange(P)[:, None])
    c[:, C_HM1] = c[:, C_HIND + 1] - 1

    o = np.zeros((BUCKETS + 1, O_END), np.float32)
    dist = np.arange(VLEN) - (P - 1)
    for n in range(4):
        ok = dist >= 0
        if n:
            d = DIL[n - 1]
            ok = ok & (dist % d == 0) & (dist <= P * d)
        b = np.where(ok, _bucket(dist), BUCKETS)
        o[b, O_TOE + n * VLEN + np.arange(VLEN)] = 1
    pos = np.arange(PAST)
    o[_bucket(PAST - pos), O_SMP + pos] = 1
    for g, d in enumerate(DIL):
        o[_bucket((P - np.arange(P)) * d), O_SMP + PAST + g * P + np.arange(P)] = 1
    o[0, O_ZERO:O_ZERO + NB] = 1
    return c, o, np.full((1, HALL), NEG, np.float32)


def kernel(**inputs):
    import numpy as _np
    import concourse.bacc as _bacc
    from concourse import mybir as _mybir
    from concourse.bass_utils import run_bass_kernel_spmd as _run

    nc = _bacc.Bacc("TRN2", target_bir_lowering=False, num_devices=1)
    arrays, args = {}, []
    given = {n: _np.ascontiguousarray(inputs[n]) for n in _INS}
    given.update(zip(("consts", "onehots", "negrow"), _constants()))
    for name, a in given.items():
        arrays[f"in_{name}_dram"] = a
        args.append(nc.dram_tensor(f"in_{name}_dram", a.shape, _mybir.dt.from_np(a.dtype), kind="ExternalInput").ap())
    for i, shape in enumerate(_OUTS):
        args.append(nc.dram_tensor(f"out_{i}_dram", shape, F32, kind="ExternalOutput").ap())
    trunk(nc, *args)
    r = _run(nc, [arrays], core_ids=[0])
    return tuple(r.results[0][f"out_{i}_dram"] for i in range(len(_OUTS)))
```
